# Optimizing a Trainium2 kernel written in Bass

```python
import jax
import jax.numpy as jnp
from jax import lax
import numpy as np

D_MODEL = 1024
BATCH = 1
SEQ = 256
DEPTH = 2
DEC_BATCH = 8
DEC_SEQ = 1
PAST_LEN = 2048
PAGE_SIZE = 128

N_MIXERS = 2
N_RWKV = (DEPTH + 1) // 2
N_MLA = DEPTH // 2
RW_HEAD = 64
RW_HEADS = D_MODEL // RW_HEAD
RW_DECAY_LORA = 64
RW_AAA_LORA = 64
RW_MV_LORA = 32
RW_GATE_LORA = 128
RW_GN_EPS = 64e-5
MLA_HEADS = 16
MLA_Q_LORA = 384
MLA_KV_LORA = 256
MLA_NOPE = 64
MLA_ROPE = 32
MLA_V = 64
MLA_SCALE = (MLA_NOPE + MLA_ROPE) ** -0.5
ROPE_THETA = 10000.0
Q_BLOCK = 128
PEER_HEADS = 8
PEER_N_KEYS = 128
PEER_N_EXPERTS = PEER_N_KEYS * PEER_N_KEYS
PEER_TOPK = 16
PEER_D_KEY = 256
PEER_BLOCK = 128
NORM_EPS = 1e-6

kernel_name = 'rwkv7_mla_peer_hybrid_step'

F32 = jnp.float32

def rms_norm(x, g):
    xf = x.astype(F32)
    y = xf * lax.rsqrt(jnp.mean(xf * xf, axis=-1, keepdims=True) + NORM_EPS)
    return y.astype(x.dtype) * g

def head_group_norm(y, w, b):
    B, T = y.shape[:2]
    yf = y.astype(F32)
    yc = yf - jnp.mean(yf, axis=-1, keepdims=True)
    var = jnp.mean(yc * yc, axis=-1, keepdims=True)
    yn = (yc * lax.rsqrt(var + RW_GN_EPS)).astype(y.dtype).reshape(B, T, D_MODEL)
    return yn * w + b

def wkv7_scan(r, decay, k, v, kk, a, s0):
    xs = tuple(jnp.moveaxis(t.astype(F32), 1, 0) for t in (r, decay, k, v, kk, a))

    def step(s, inp):
        r_t, w_t, k_t, v_t, kk_t, a_t = inp
        s_kk = jnp.einsum('bhvk,bhk->bhv', s, kk_t)
        s = (s * w_t[:, :, None, :]
             - s_kk[..., None] * (kk_t * a_t)[:, :, None, :]
             + v_t[..., None] * k_t[:, :, None, :])
        return s, jnp.einsum('bhvk,bhk->bhv', s, r_t)

    s, ys = lax.scan(step, s0.astype(F32), xs)
    return jnp.moveaxis(ys, 0, 1).astype(r.dtype), s.astype(s0.dtype)

def rwkv7_mix(h, shift_prev, wkv0, v_first, vres, mu, w_in, w0, w1, w2, a0, a1, a2,
              g1, g2, k_k, k_a, r_k, ln_w, ln_b, w_out):
    B, T, _ = h.shape
    prev = jnp.concatenate([shift_prev[:, None, :].astype(h.dtype), h[:, :-1]], axis=1)
    xx = prev - h
    xr, xw, xk, xv, xa, xg = [h + xx * mu[m] for m in range(6)]
    r, k, v = jnp.einsum('gbtd,gde->gbte', jnp.stack([xr, xk, xv]), w_in)
    w_log = -jax.nn.softplus(-(w0 + jnp.tanh(xw @ w1) @ w2).astype(F32)) - 0.5
    decay = jnp.exp(-jnp.exp(w_log))
    a = jax.nn.sigmoid(a0 + (xa @ a1) @ a2)
    g = jax.nn.sigmoid(xg @ g1) @ g2
    if vres is not None:
        v0, v1, v2 = vres
        v = v + (v_first - v) * jax.nn.sigmoid(v0 + (xv @ v1) @ v2)

    def heads(t):
        return t.reshape(B, T, RW_HEADS, RW_HEAD)

    kk = heads(k * k_k).astype(F32)
    kk = kk * lax.rsqrt(jnp.maximum(jnp.sum(kk * kk, axis=-1, keepdims=True), 1e-24))
    k = k * (1.0 + (a - 1.0) * k_a)
    r_h, k_h, v_h = heads(r), heads(k), heads(v)
    y, wkv = wkv7_scan(r_h, heads(decay), k_h, v_h, kk, heads(a), wkv0)
    y = head_group_norm(y, ln_w, ln_b)
    bonus = jnp.sum(r_h * k_h * r_k, axis=-1, keepdims=True) * v_h
    y = y + bonus.reshape(B, T, D_MODEL)
    return (y * g) @ w_out, v, h[:, -1], wkv

def rope_tables(pos):
    inv = ROPE_THETA ** (-jnp.arange(0, MLA_ROPE, 2, dtype=F32) / MLA_ROPE)
    ang = pos.astype(F32)[:, None] * inv[None, :]
    return jnp.cos(ang), jnp.sin(ang)

def apply_rope(x, cos, sin):
    half = x.shape[-1] // 2
    x1 = x[..., :half].astype(F32)
    x2 = x[..., half:].astype(F32)
    return jnp.concatenate([x1 * cos - x2 * sin, x2 * cos + x1 * sin], axis=-1).astype(x.dtype)

def split_kvb(w_kvb):
    w = w_kvb.reshape(MLA_KV_LORA, MLA_HEADS, MLA_NOPE + MLA_V)
    return w[..., :MLA_NOPE], w[..., MLA_NOPE:]

def mla_keys(ckv, w_uk, kn_nope):
    return rms_norm(jnp.einsum('...c,chd->...hd', ckv, w_uk), kn_nope)

def mla_scores(q_nope, q_pe, k_nope, k_pe):
    s = (jnp.einsum('bqhd,bkhd->bhqk', q_nope, k_nope)
         + jnp.einsum('bqhr,bkr->bhqk', q_pe, k_pe))
    return s.astype(F32) * MLA_SCALE

def mla_prompt_attention(q_nope, q_pe, k_nope, k_pe, v):
    B, S = q_nope.shape[:2]
    k_pos = jnp.arange(S)

    def block(start):
        qn = lax.dynamic_slice_in_dim(q_nope, start, Q_BLOCK, axis=1)
        qp = lax.dynamic_slice_in_dim(q_pe, start, Q_BLOCK, axis=1)
        s = mla_scores(qn, qp, k_nope, k_pe)
        q_pos = start + jnp.arange(Q_BLOCK)
        s = jnp.where(k_pos[None, :] <= q_pos[:, None], s, -jnp.inf)
        p = jax.nn.softmax(s, axis=-1)
        return jnp.einsum('bhqk,bkhv->bqhv', p.astype(v.dtype), v)

    o = lax.map(block, jnp.arange(0, S, Q_BLOCK))
    return jnp.moveaxis(o, 0, 1).reshape(B, S, MLA_HEADS, MLA_V)

def mla_sample_attention(q_nope, q_pe, ckv_new, k_nope_new, k_pe_new, pool_ckv, pool_kpe,
                         page_table, w_uk, w_uv, kn_nope):
    B, T = q_nope.shape[:2]

    def merge(carry, s, ckv):
        m, l, acc = carry
        m_new = jnp.maximum(m, jnp.max(s, axis=-1))
        corr = jnp.exp(m - m_new)
        p = jnp.exp(s - m_new[..., None])
        l = l * corr + jnp.sum(p, axis=-1)
        acc = acc * corr[..., None] + jnp.einsum('bhqk,bkc->bhqc', p, ckv.astype(F32))
        return (m_new, l, acc)

    def page_step(carry, p_idx):
        phys = page_table[:, p_idx]
        ckv = pool_ckv[phys]
        s = mla_scores(q_nope, q_pe, mla_keys(ckv, w_uk, kn_nope), pool_kpe[phys])
        return merge(carry, s, ckv), None

    init = (jnp.full((B, MLA_HEADS, T), -jnp.inf, F32),
            jnp.zeros((B, MLA_HEADS, T), F32),
            jnp.zeros((B, MLA_HEADS, T, MLA_KV_LORA), F32))
    carry, _ = lax.scan(page_step, init, jnp.arange(page_table.shape[1]))
    s = mla_scores(q_nope, q_pe, k_nope_new, k_pe_new)
    s = jnp.where(jnp.tril(jnp.ones((T, T), dtype=bool)), s, -jnp.inf)
    _, l, acc = merge(carry, s, ckv_new)
    o = jnp.einsum('bhqc,chv->bqhv', acc / l[..., None], w_uv.astype(F32))
    return o.astype(q_nope.dtype)

def mla_mix(h, cos, sin, past, w_in, q_norm, kv_norm, w_qb, w_kvb, qn_nope, qn_rope,
            kn_nope, kn_rope, w_out):
    B, T, _ = h.shape
    proj = h @ w_in
    cq = rms_norm(proj[..., :MLA_Q_LORA], q_norm)
    ckv = rms_norm(proj[..., MLA_Q_LORA:MLA_Q_LORA + MLA_KV_LORA], kv_norm)
    k_pe = apply_rope(rms_norm(proj[..., MLA_Q_LORA + MLA_KV_LORA:], kn_rope), cos, sin)
    q = (cq @ w_qb).reshape(B, T, MLA_HEADS, MLA_NOPE + MLA_ROPE)
    q_nope = rms_norm(q[..., :MLA_NOPE], qn_nope)
    q_pe = apply_rope(rms_norm(q[..., MLA_NOPE:], qn_rope), cos[:, None], sin[:, None])
    w_uk, w_uv = split_kvb(w_kvb)
    k_nope = mla_keys(ckv, w_uk, kn_nope)
    if past is None:
        v = jnp.einsum('btc,chv->bthv', ckv, w_uv)
        o = mla_prompt_attention(q_nope, q_pe, k_nope, k_pe, v)
    else:
        pool_ckv, pool_kpe, page_table = past
        o = mla_sample_attention(q_nope, q_pe, ckv, k_nope, k_pe, pool_ckv, pool_kpe,
                                 page_table, w_uk, w_uv, kn_nope)
    return o.reshape(B, T, MLA_HEADS * MLA_V) @ w_out, ckv, k_pe

def peer_ffn(x, w_q, sub_keys, u_tab, v_tab):
    shape = x.shape
    xt = x.reshape(-1, D_MODEL)
    n = xt.shape[0]
    n_pad = (-n) % PEER_BLOCK
    blocks = jnp.pad(xt, ((0, n_pad), (0, 0))).reshape(-1, PEER_BLOCK, D_MODEL)
    n_cand = PEER_TOPK * PEER_TOPK

    def block(xb):
        q = (xb @ w_q).reshape(PEER_BLOCK, PEER_HEADS, 2, PEER_D_KEY // 2)
        s = jnp.einsum('thcd,cnd->thcn', q, sub_keys).astype(F32)
        s1, i1 = lax.top_k(s[:, :, 0], PEER_TOPK)
        s2, i2 = lax.top_k(s[:, :, 1], PEER_TOPK)
        cand_s = (s1[..., :, None] + s2[..., None, :]).reshape(PEER_BLOCK, PEER_HEADS, n_cand)
        cand_e = (i1[..., :, None] * PEER_N_KEYS + i2[..., None, :]).reshape(PEER_BLOCK, PEER_HEADS, n_cand)
        top_s, top_pos = lax.top_k(cand_s, PEER_TOPK)
        experts = jnp.take_along_axis(cand_e, top_pos, axis=-1)
        gate = jax.nn.softmax(top_s, axis=-1)
        act = jax.nn.gelu(jnp.einsum('thkd,td->thk', u_tab[experts], xb).astype(F32))
        return jnp.einsum('thk,thkd->td', (gate * act).astype(xb.dtype), v_tab[experts])

    y = lax.map(block, blocks).reshape(-1, D_MODEL)[:n]
    return y.reshape(shape)

def setup_inputs(seed: int = 0) -> dict:
    key = jax.random.key(seed)
    keys = iter(jax.random.split(key, 64))

    def nrm(shape, scale):
        return jax.random.normal(next(keys), shape, F32) * scale

    def gain(shape):
        return 1.0 + nrm(shape, 0.02)

    D = D_MODEL
    n_pages = PAST_LEN // PAGE_SIZE
    n_used = DEC_BATCH * n_pages
    n_pool = (5 * n_used + 3) // 4
    page_table = jax.random.permutation(next(keys), n_pool)[:n_used].reshape(DEC_BATCH, n_pages).astype(jnp.int32)
    nv = max(N_RWKV - 1, 0)
    return {
        'x_prompt': nrm((BATCH, SEQ, D), 1.0),
        'x_sample': nrm((DEC_BATCH, DEC_SEQ, D), 1.0),
        'cache_ckv': nrm((N_MLA, n_pool, PAGE_SIZE, MLA_KV_LORA), 1.0),
        'cache_kpe': nrm((N_MLA, n_pool, PAGE_SIZE, MLA_ROPE), 1.0),
        'page_table': page_table,
        'state_wkv': nrm((N_RWKV, DEC_BATCH, RW_HEADS, RW_HEAD, RW_HEAD), 0.3),
        'state_shift': nrm((N_RWKV, DEC_BATCH, D), 1.0),
        'norm_mix': gain((DEPTH, D)),
        'norm_ffn': gain((DEPTH, D)),
        'rw_mu': jax.random.uniform(next(keys), (N_RWKV, 6, D), F32),
        'rw_w_in': nrm((N_RWKV, 3, D, D), D ** -0.5),
        'rw_w0': nrm((N_RWKV, D), 0.5),
        'rw_w1': nrm((N_RWKV, D, RW_DECAY_LORA), D ** -0.5),
        'rw_w2': nrm((N_RWKV, RW_DECAY_LORA, D), 0.5 * RW_DECAY_LORA ** -0.5),
        'rw_a0': nrm((N_RWKV, D), 0.5),
        'rw_a1': nrm((N_RWKV, D, RW_AAA_LORA), D ** -0.5),
        'rw_a2': nrm((N_RWKV, RW_AAA_LORA, D), RW_AAA_LORA ** -0.5),
        'rw_v0': nrm((nv, D), 0.5),
        'rw_v1': nrm((nv, D, RW_MV_LORA), D ** -0.5),
        'rw_v2': nrm((nv, RW_MV_LORA, D), RW_MV_LORA ** -0.5),
        'rw_g1': nrm((N_RWKV, D, RW_GATE_LORA), D ** -0.5),
        'rw_g2': nrm((N_RWKV, RW_GATE_LORA, D), RW_GATE_LORA ** -0.5),
        'rw_k_k': 1.0 + nrm((N_RWKV, D), 0.1),
        'rw_k_a': 1.0 + nrm((N_RWKV, D), 0.1),
        'rw_r_k': nrm((N_RWKV, RW_HEADS, RW_HEAD), 0.1),
        'rw_ln_w': gain((N_RWKV, D)),
        'rw_ln_b': nrm((N_RWKV, D), 0.02),
        'rw_w_out': nrm((N_RWKV, D, D), D ** -0.5),
        'mla_w_in': nrm((N_MLA, D, MLA_Q_LORA + MLA_KV_LORA + MLA_ROPE), D ** -0.5),
        'mla_q_norm': gain((N_MLA, MLA_Q_LORA)),
        'mla_kv_norm': gain((N_MLA, MLA_KV_LORA)),
        'mla_w_qb': nrm((N_MLA, MLA_Q_LORA, MLA_HEADS * (MLA_NOPE + MLA_ROPE)), MLA_Q_LORA ** -0.5),
        'mla_w_kvb': nrm((N_MLA, MLA_KV_LORA, MLA_HEADS * (MLA_NOPE + MLA_V)), MLA_KV_LORA ** -0.5),
        'mla_qn_nope': gain((N_MLA, MLA_NOPE)),
        'mla_qn_rope': gain((N_MLA, MLA_ROPE)),
        'mla_kn_nope': gain((N_MLA, MLA_NOPE)),
        'mla_kn_rope': gain((N_MLA, MLA_ROPE)),
        'mla_w_out': nrm((N_MLA, MLA_HEADS * MLA_V, D), (MLA_HEADS * MLA_V) ** -0.5),
        'peer_w_q': nrm((DEPTH, D, PEER_HEADS * PEER_D_KEY), D ** -0.5),
        'peer_sub_keys': nrm((DEPTH, 2, PEER_N_KEYS, PEER_D_KEY // 2), (PEER_D_KEY // 2) ** -0.5),
        'peer_u': nrm((DEPTH, PEER_N_EXPERTS, D), D ** -0.5),
        'peer_v': nrm((DEPTH, PEER_N_EXPERTS, D), 0.2),
    }

def reference(x_prompt, x_sample, cache_ckv, cache_kpe, page_table, state_wkv, state_shift,
              norm_mix, norm_ffn,
              rw_mu, rw_w_in, rw_w0, rw_w1, rw_w2, rw_a0, rw_a1, rw_a2, rw_v0, rw_v1, rw_v2,
              rw_g1, rw_g2, rw_k_k, rw_k_a, rw_r_k, rw_ln_w, rw_ln_b, rw_w_out,
              mla_w_in, mla_q_norm, mla_kv_norm, mla_w_qb, mla_w_kvb, mla_qn_nope, mla_qn_rope,
              mla_kn_nope, mla_kn_rope, mla_w_out,
              peer_w_q, peer_sub_keys, peer_u, peer_v):

    def trunk(x, pos, shift_init, wkv_init, past):
        cos, sin = rope_tables(pos)
        v_first = None
        shifts, wkvs, ckvs, kpes = [], [], [], []
        for i in range(DEPTH):
            j = i // N_MIXERS
            h = rms_norm(x, norm_mix[i])
            if i % N_MIXERS == 0:
                vres = None if j == 0 else (rw_v0[j - 1], rw_v1[j - 1], rw_v2[j - 1])
                out, v, s_last, wkv_last = rwkv7_mix(
                    h, shift_init[j], wkv_init[j], v_first, vres, rw_mu[j], rw_w_in[j],
                    rw_w0[j], rw_w1[j], rw_w2[j], rw_a0[j], rw_a1[j], rw_a2[j],
                    rw_g1[j], rw_g2[j], rw_k_k[j], rw_k_a[j], rw_r_k[j],
                    rw_ln_w[j], rw_ln_b[j], rw_w_out[j])
                if j == 0:
                    v_first = v
                shifts.append(s_last)
                wkvs.append(wkv_last)
            else:
                layer_past = None if past is None else (past[0][j], past[1][j], past[2])
                out, ckv, kpe = mla_mix(
                    h, cos, sin, layer_past, mla_w_in[j], mla_q_norm[j], mla_kv_norm[j],
                    mla_w_qb[j], mla_w_kvb[j], mla_qn_nope[j], mla_qn_rope[j],
                    mla_kn_nope[j], mla_kn_rope[j], mla_w_out[j])
                ckvs.append(ckv)
                kpes.append(kpe)
            x = x + out
            x = x + peer_ffn(rms_norm(x, norm_ffn[i]), peer_w_q[i], peer_sub_keys[i],
                             peer_u[i], peer_v[i])
        return x, jnp.stack(ckvs), jnp.stack(kpes), jnp.stack(wkvs), jnp.stack(shifts)

    b_p, s_p = x_prompt.shape[:2]
    shift0 = jnp.zeros((N_RWKV, b_p, D_MODEL), x_prompt.dtype)
    wkv0 = jnp.zeros((N_RWKV, b_p, RW_HEADS, RW_HEAD, RW_HEAD), state_wkv.dtype)
    y_prompt, ckv_prompt, kpe_prompt, wkv_prompt, shift_prompt = trunk(
        x_prompt, jnp.arange(s_p), shift0, wkv0, None)

    past_len = page_table.shape[1] * cache_ckv.shape[2]
    pos_sample = past_len + jnp.arange(x_sample.shape[1])
    y_sample, ckv_sample, kpe_sample, wkv_sample, shift_sample = trunk(
        x_sample, pos_sample, state_shift, state_wkv, (cache_ckv, cache_kpe, page_table))

    return (y_prompt, y_sample, ckv_prompt, kpe_prompt, wkv_prompt, shift_prompt,
            ckv_sample, kpe_sample, wkv_sample, shift_sample)


_drawn_inputs = setup_inputs


def setup_inputs(seed=0):
    import zlib

    import numpy as np

    out = dict(_drawn_inputs(seed))
    spreads = {}
    factors = {'cache_kpe': 3.03,
     'norm_ffn': 2.852,
     'rw_k_k': 2.955,
     'rw_ln_w': 3.205,
     'rw_ln_b': 3.047,
     'mla_q_norm': 8.0,
     'mla_kv_norm': 2.756,
     'mla_qn_nope': 8.0,
     'mla_qn_rope': 30.09,
     'mla_kn_nope': 8.0}
    for name, (base, spread) in spreads.items():
        noise = np.random.default_rng([zlib.crc32(name.encode()), seed]).standard_normal(out[name].shape)
        drawn = base * np.exp(spread * noise) if base else spread * noise
        out[name] = jnp.asarray(drawn.astype(out[name].dtype))
    for name, factor in factors.items():
        out[name] = (out[name] * factor).astype(out[name].dtype)
    return out
```

```python
from contextlib import ExitStack

import numpy as np

import concourse.bass as bass
from concourse import mybir

F32 = mybir.dt.float32
I32 = mybir.dt.int32
U32 = mybir.dt.uint32
ALU = mybir.AluOpType
ACT = mybir.ActivationFunctionType
AX = mybir.AxisListType

P = 128
D = 1024
DC = D // P
NP_ = 256
NS = 8
T = NP_ + NS
HEADS = 16
CH = 64
NCH = NP_ // CH
QL, KVL, ROPE = 384, 256, 32
QC = QL // P
SCALE = (64 + 32) ** -0.5
EPS = 1e-6
GN_EPS = 64e-5
NPAGE = 16
PAGES = NS * NPAGE
POOL = (5 * PAGES + 3) // 4
PH = 8
TOPK = 16
TT = [(0, 128), (128, 128), (256, 8)]
NEG = -1e30
VERY_NEG = -3e38

RING = 8
TILES = {}
_n = 0
for _name, _count in [("r", 8), ("k", 8), ("v", 8), ("w1", 1), ("a1", 1), ("g1", 1), ("w2", 1), ("a2", 1), ("g2", 1),
                      ("rw_out", 8), ("wq0", 16), ("peer0", 256),
                      ("mla_in", 6), ("qb", 12), ("mla_out", 8), ("wq1", 16), ("peer1", 256)]:
    TILES[_name] = _n
    _n += _count
NTILES = _n
assert NTILES % RING == 0
GR = 2
NGROUP = P // GR

VECS = ["norm_mix0", "norm_mix1", "norm_ffn0", "norm_ffn1", "mu0", "mu1", "mu2", "mu3", "mu4", "mu5",
        "w0", "a0", "k_k", "k_a", "r_k", "ln_w", "ln_b"]
VCOL = {n: i * DC for i, n in enumerate(VECS)}
for _n2, _w in [("q_norm", 3), ("kv_norm", 2), ("qn_nope", 1), ("qn_rope", 1), ("kn_nope", 1), ("kn_rope", 1)]:
    VCOL[_n2] = max(VCOL.values()) + (DC if len(VCOL) == len(VECS) else _prev)
    _prev = _w
NV = VCOL["kn_rope"] + 1

CONSTS = ["ident", "ones", "bd64", "bd32", "rot", "iota", "stack", "half0", "half1", "quar0", "quar1", "quar2", "quar3"]
CCOL = {n: i * P for i, n in enumerate(CONSTS)}
CCOL["amask"] = len(CONSTS) * P
NCONST = (len(CONSTS) + 3) * P
WMASKS = ["strict", "incl"] + [f"level{i}" for i in range(6)]


def const_arrays():
    i = np.arange(P)
    eye = np.eye(P, dtype=np.float32)
    rot = np.zeros((P, P), np.float32)
    for m in range(P):
        if m % 32 < 16:
            rot[m + 16, m] = -1.0
        else:
            rot[m - 16, m] = 1.0
    causal = np.where(i[None, :] <= i[:, None], 0.0, NEG).astype(np.float32)
    mats = {"ident": eye, "ones": np.ones((P, P)), "bd64": i[:, None] // 64 == i[None, :] // 64,
            "bd32": i[:, None] // 32 == i[None, :] // 32, "rot": rot, "stack": i[:, None] % 64 == i[None, :], "iota": np.broadcast_to(i, (P, P))}
    for h in range(2):
        mats[f"half{h}"] = np.broadcast_to((i // 64 == h)[:, None], (P, P))
    for h in range(4):
        mats[f"quar{h}"] = np.broadcast_to((i // 32 == h)[:, None], (P, P))
    cols = [mats[n] for n in CONSTS] + [causal, np.zeros((P, P)), causal]
    s, t = i[:, None], i[None, :]
    same = s // CH == t // CH
    wm = [same & (s < t), same & (s <= t)]
    for lev in range(6):
        b = 1 << lev
        wm.append(-1.0 * ((s // (2 * b) == t // (2 * b)) & (s // b % 2 == 0) & (t // b % 2 == 1)))
    pos = np.concatenate([np.arange(NP_), np.full(NS, NPAGE * P)]).astype(np.float32)
    inv = np.float32(10000.0) ** (-np.arange(0, ROPE, 2, dtype=np.float32) / np.float32(ROPE))
    ang = (pos[None, :] * inv[i % 16][:, None].astype(np.float32)).astype(np.float32)
    rope = np.stack([np.cos(ang), np.sin(ang)], 1)
    f = lambda x: np.ascontiguousarray(np.concatenate([np.asarray(y, np.float32) for y in x], 1))
    return f(cols), f(wm), np.ascontiguousarray(rope.astype(np.float32))


class Seen:

    def __init__(self, eng):
        self.eng, self.n = eng, {}

    def next(self, sem, k=1):
        v = self.n.get(id(sem), 0) + k
        self.n[id(sem)] = v
        self.eng.wait_ge(sem, v)

    def passed(self, sem, k):
        self.n[id(sem)] = self.n.get(id(sem), 0) + k

    def count(self, sem):
        return self.n.get(id(sem), 0)


def build(nc, x_t, shift_t, vecs, consts, wmasks, rope, wstream, sub_keys, mla_w, page_table, cache_t, cache_n,
          state, y_out, ckv_out, kpe_out, wkv_p_out, shift_out, wkv_s_out):
    ctx = ExitStack()
    with ctx:
        def sb(name, cols, dt=F32):
            return ctx.enter_context(nc.sbuf_tensor(name, [P, cols], dt))

        def sem(name):
            return ctx.enter_context(nc.semaphore(name))

        ARENA = 35240
        arena = sb("arena", ARENA)
        ring = sb("ring", RING * D)
        xbuf = sb("xbuf", DC * T)
        xnbuf = sb("xnbuf", DC * T)
        hbuf = sb("hbuf", 2 * GR * T)
        cst = sb("cst", NCONST)
        vec = sb("vec", NV)
        skb = sb("skb", 4 * P)
        idxb = sb("idxb", 3 * T)
        rsb = sb("rsb", 3 * T)
        ps = ctx.enter_context(nc.psum_tensor("ps", [P, 8, 512], F32))
        scr_in = nc.dram_tensor("scr_in", [6, NS, D], F32).ap()
        scr_y = nc.dram_tensor("scr_y", [NS, D], F32).ap()

        xT = xbuf[:, :].rearrange("p (c t) -> p c t", c=DC)
        xn = xnbuf[:, :].rearrange("p (c t) -> p c t", c=DC)

        def C(name, n=P):
            return cst[:, CCOL[name]:CCOL[name] + n]

        def V(name, i=0, n=1):
            return vec[:, VCOL[name] + i:VCOL[name] + i + n]

        def vb(name, n=T):
            return V(name, 0, DC).unsqueeze(2).broadcast_to([P, DC, n])

        def slot(n):
            s = n % RING
            return ring[:, s * D:(s + 1) * D].rearrange("p (c m) -> p c m", c=DC)

        top = [0]

        def A(cols, *dims):
            a = arena[:, top[0]:top[0] + cols]
            top[0] += cols
            assert top[0] <= ARENA, top[0]
            if len(dims) == 2:
                return a.rearrange("p (a b) -> p a b", b=dims[1])
            if len(dims) == 3:
                return a.rearrange("p (a b c) -> p a b c", b=dims[1], c=dims[2])
            return a

        N3 = DC * T
        r_t, k_t, v_t, ld_t, a_t, g_t = (A(N3, DC, T) for _ in range(6))
        kk_t = A(N3, DC, T)
        bon_t = A(N3, DC, T)
        mix = [A(N3, DC, T) for _ in range(2)]
        xx = A(N3, DC, T)
        tmp_t = A(N3, DC, T)
        Rb = A(DC * NP_, DC, NP_)
        wm = A(8 * P, 8, P)
        smp = A(6 * DC * NS, 6, DC, NS)
        lam = A(DC * NCH, DC, NCH)
        lw, la, lg = (A(T) for _ in range(3))
        smp_row = A(6 * 64, 6, 64)
        shift_sb = lw[:, 0:DC * NS].rearrange("p (c b) -> p c b", c=DC)
        rw_top = top[0]

        def over(view, n, *dims):
            a = view.rearrange("p c t -> p (c t)")[:, 0:n]
            if len(dims) == 2:
                return a.rearrange("p (a b) -> p a b", b=dims[1])
            if len(dims) == 3:
                return a.rearrange("p (a b c) -> p a b c", b=dims[1], c=dims[2])
            return a

        cum = [over(mix[0], DC * NP_, DC, NP_), over(mix[1], DC * NP_, DC, NP_)]
        Kb = over(xx, DC * NP_, DC, NP_)
        Bb = over(tmp_t, DC * NP_, DC, NP_)
        kb = cum[0]
        y_t = r_t
        ETi = over(xx, DC * NCH * 64, DC, NCH, 64)
        Hk = over(mix[0], DC * NCH * 64, DC, NCH, 64)
        pt = [kk_t.rearrange("p c t -> p (c t)")[:, i * 512:(i + 1) * 512] for i in range(4)] + \
             [a_t.rearrange("p c t -> p (c t)")[:, i * 512:(i + 1) * 512] for i in range(4)] + \
             [ld_t.rearrange("p c t -> p (c t)")[:, i * 512:(i + 1) * 512] for i in range(4)]
        LT, MTm, ArkT, ArbT, Xs, XTs, Zs, RHS, BKrow, nWU, NTl0, NTl1 = pt
        NTl = [NTl0, NTl1]
        q4 = lambda a: a.rearrange("p (q n) -> p q n", q=4)
        mis = mix[1].rearrange("p c t -> p (c t)")
        Vrow = mis[:, 0:256].rearrange("p (j h v) -> p j h v", j=2, h=2)
        Pst = mis[:, 256:256 + 512].rearrange("p (c v) -> p c v", c=DC)
        st_q = [k_t.rearrange("p c t -> p (c t)")[:, i * D:(i + 1) * D].rearrange("p (v k) -> p v k", v=16) for i in range(2)]
        vflat = hbuf
        st_tmp = vflat[:, 0:D].rearrange("p (v k) -> p v k", v=16)
        skk = rsb[:, 0:16]
        y_smp = rsb[:, 64:128]
        top[0] = rw_top
        rows_sb = [A(2 * D)[0:NS, :], A(2 * D)[0:NS, :], Rb.rearrange("p c t -> p (c t)")[0:NS, :]]

        top[0] = 0
        G = arena[:, 0:P * T].rearrange("p (n t) -> p n t", n=P)
        S = A(3 * 16 * P, 3, 16, P)
        S2 = A(16 * P, 16, P)
        v16 = A(16 * TOPK, 16, TOPK)
        i16u = arena[:, top[0]:top[0] + 256].bitcast(U32).rearrange("p (g k) -> p g k", g=16)
        top[0] += 256
        i16f = A(16 * TOPK, 16, TOPK)
        cand = A(PH * 256, PH, 256)
        cand2 = A(PH * 256, PH, 256)
        eq = A(PH * 256, PH, 256)
        ts16 = A(PH * TOPK, PH, TOPK)
        posu = arena[:, top[0]:top[0] + 128].bitcast(U32).rearrange("p (g k) -> p g k", g=PH)
        top[0] += 128
        abu = arena[:, top[0]:top[0] + 256].bitcast(U32).rearrange("p (two n) -> p two n", two=2)
        top[0] += 256
        abf = A(2 * 128, 2, 128)
        sel = A(3 * 3 * P, 3, 3, P)
        smax = A(PH, PH, 1)
        qb = [A(T), A(T)]
        idx = idxb[:, :].rearrange("p (k t) -> p k t", k=3)
        hset = [hbuf[:, s * 512:(s + 1) * 512].rearrange("p (k u n) -> p k u n", k=2, u=2) for s in range(2)]
        hg = hbuf[:, :].rearrange("p (g t) -> p g t", t=T)

        top[0] = 0
        w_uk = A(2 * D, 2, D)
        w_uv = A(2 * D, 2, D)
        w_ukT = A(DC * KVL, DC, KVL)
        cs = A(2 * T, 2, T)
        cq = A(3 * T, 3, T)
        ckv = A(2 * T, 2, T)
        kp = A(T)
        qn = A(N3, DC, T)
        kn = A(N3, DC, T)
        qr = A(4 * T, 4, T)
        sqb = A(N3, DC, T)
        rs8 = A(N3, DC, T)
        vr = A(2 * D, 2, D)
        o_t = A(N3, DC, T)
        qm = [A(512, 2, 256) for _ in range(2)]
        Sm = [A(384) for _ in range(2)]
        PTs = [A(384) for _ in range(2)]
        mxl = [A(8) for _ in range(2)]
        o_row = A(2 * D, 2, D)
        qgm = A(DC * 2 * NS, DC, 2, NS)
        qp = A(2 * NS * HEADS, 2, NS, HEADS)
        qrz = A(NS * HEADS, NS, HEADS)
        prodn = A(DC * NS, DC, NS)
        prodr = A(4 * NS, 4, NS)
        NPG = PAGES * HEADS
        SN = A(2 * NPG, PAGES, 2 * HEADS)
        SS = A(NPG, PAGES, HEADS)
        sqp = [o_row[:, j, :] for j in range(2)]
        small = A(10 * P, 10, P)
        cpT = [x.rearrange("p (a b) -> p a b", a=3) for x in Sm + PTs]
        accT = A(2 * P, 2, NS, HEADS)
        cnew = A(2 * P, 2, NS, HEADS)
        PR = rs8.rearrange("p c t -> p (c t)")[:, 0:NPG].rearrange("p (g h) -> p g h", h=HEADS)
        cpN = [sqb.rearrange("p c t -> p (c t)")[:, i * KVL:(i + 1) * KVL] for i in range(8)]
        ptab = ctx.enter_context(nc.sbuf_tensor("ptab", [1, PAGES], I32))

        consts_in = sem("consts_in")
        slot_in = [sem(f"slot_in{i}") for i in range(RING)]
        tile_used = sem("tile_used")
        bank_free = [sem(f"bank_free{i}") for i in range(8)]
        for_act = sem("for_act")
        for_dve = sem("for_dve")
        nat_free = sem("nat_free")
        dve_step = sem("dve_step")
        act_step = sem("act_step")
        sq_ready = sem("sq_ready")
        rsq_in = sem("rsq_in")
        rsq_out = sem("rsq_out")
        xn_ready = sem("xn_ready")
        mix_ready = sem("mix_ready")
        lora_ready = sem("lora_ready")
        stat_ready = sem("stat_ready")
        proj_copied = sem("proj_copied")
        smp_ready = sem("smp_ready")
        smp_rows = sem("smp_rows")
        smp_out = sem("smp_out")
        smp_back = sem("smp_back")
        st_in = [sem(f"st_in{i}") for i in range(2)]
        st_done = sem("st_done")
        st_out = sem("st_out")
        ysm_out = sem("ysm_out")
        ysm_back = sem("ysm_back")
        ysm_T = sem("ysm_T")
        ld_scaled = sem("ld_scaled")
        cum_ready = sem("cum_ready")
        e_ready = sem("e_ready")
        ops_ready = sem("ops_ready")
        rows_act = sem("rows_act")
        rows_dve = sem("rows_dve")
        nt_ready = sem("nt_ready")
        lt_ready = sem("lt_ready")
        z_ready = sem("z_ready")
        x_ready = sem("x_ready")
        xt_ready = sem("xt_ready")
        rhs_ready = sem("rhs_ready")
        nwu_ready = sem("nwu_ready")
        ab_ready = sem("ab_ready")
        pair_done = sem("pair_done")
        state_ready = sem("state_ready")
        y_ready = sem("y_ready")
        yg_ready = sem("yg_ready")
        x_added = sem("x_added")
        q_copied = sem("q_copied")
        s_copied = sem("s_copied")
        sel_ready = sem("sel_ready")
        idx_ready = sem("idx_ready")
        oh_ready = sem("oh_ready")
        oh_used = sem("oh_used")
        g_stored = sem("g_stored")
        gelu_done = sem("gelu_done")
        h_ready = sem("h_ready")
        h_used = sem("h_used")
        shift_sent = sem("shift_sent")
        wkv_sent = sem("wkv_sent")
        lat_sent = sem("lat_sent")
        y_sent = sem("y_sent")
        pr_exp = sem("pr_exp")
        gate_in = sem("gate_in")
        gate_exp = sem("gate_exp")
        smp_decay = sem("smp_decay")
        mla_in = sem("mla_in")
        kp_ready = sem("kp_ready")
        lat_ready = sem("lat_ready")
        heads_ready = sem("heads_ready")
        qm_ready = sem("qm_ready")
        neg_ready = sem("neg_ready")
        p_ready = sem("p_ready")
        pt_ready = sem("pt_ready")
        o_ready = sem("o_ready")
        oT_copied = sem("oT_copied")
        qs_ready = sem("qs_ready")
        qp_ready = sem("qp_ready")
        page_in = [sem(f"page_in{i}") for i in range(4)]
        page_used = sem("page_used")
        sqp_ready = sem("sqp_ready")
        sqp_used = sem("sqp_used")
        m1_ready = sem("m1_ready")
        dg_ready = sem("dg_ready")
        pr_in = sem("pr_in")
        pr_ready = sem("pr_ready")
        natp_in = [sem(f"natp_in{i}") for i in range(8)]
        natp_used = sem("natp_used")
        acc_ready = sem("acc_ready")
        oall_ready = sem("oall_ready")

        block = ctx.enter_context(nc.Block())
        marks = {}

        @block.sync
        def _(sp):
            w = Seen(sp)
            sp.dma_start(xbuf[:, :], x_t).then_inc(consts_in, 16)
            sp.dma_start(vec[:, :], vecs).then_inc(consts_in, 16)
            sp.dma_start(cst[:, :], consts).then_inc(consts_in, 16)
            sp.dma_start(shift_sb, shift_t).then_inc(consts_in, 16)
            sp.dma_start(skb[:, :], sub_keys).then_inc(consts_in, 16)
            sp.dma_start(wm.rearrange("p a b -> p (a b)"), wmasks).then_inc(consts_in, 16)
            sp.dma_start(ptab[:, :], page_table).then_inc(consts_in, 16)
            for n in range(RING):
                sp.dma_start(ring[:, n * D:(n + 1) * D], wstream[n, :, :]).then_inc(slot_in[n], 16)
            with sp.Fori(1, NTILES // RING) as rnd:
                for n in range(RING):
                    sp.wait_ge(tile_used, rnd * RING + (n + 1 - RING))
                    sp.dma_start(ring[:, n * D:(n + 1) * D],
                                 wstream[bass.ds(rnd * RING + n, 1), :, :].rearrange("o p n -> (o p) n")
                                 ).then_inc(slot_in[n], 16)

        @block.gpsimd
        def _(pool):
            w = Seen(pool)
            w.next(xn_ready)
            pool.dma_start(shift_out, xn[:, :, NP_ - 1:T]).then_inc(shift_sent, 16)
            for g in range(3):
                pool.wait_ge(smp_rows, 4 * (g + 1))
                pool.dma_start(scr_in[2 * g:2 * g + 2].rearrange("j b n -> b j n"),
                               rows_sb[g].rearrange("b (j n) -> b j n", j=2)).then_inc(smp_out, 16)
            pool.wait_ge(smp_out, 48)
            for j in range(6):
                pool.dma_start(smp_row[:, j, :], scr_in[j].rearrange("b (h v) -> (b h) v", h=HEADS)
                               ).then_inc(smp_back, 16)
            pool.wait_ge(ops_ready, 1)
            for qd in range(4):
                if qd >= 2:
                    pool.wait_ge(st_out, 16 * (qd - 1))
                pool.dma_start(st_q[qd % 2].rearrange("p v k -> p (v k)"), state[:, qd * D:(qd + 1) * D]).then_inc(st_in[qd % 2], 16)
                if qd >= 1:
                    pool.wait_ge(st_done, qd)
                    pool.dma_start(wkv_s_out[:, (qd - 1) * D:qd * D],
                                   st_q[(qd - 1) % 2].rearrange("p v k -> p (v k)")).then_inc(st_out, 16)
            pool.wait_ge(st_done, 4)
            pool.dma_start(wkv_s_out[:, 3 * D:4 * D], st_q[1].rearrange("p v k -> p (v k)")).then_inc(st_out, 16)
            pool.dma_start(scr_y.rearrange("b (h v) -> (b h) v", h=HEADS), y_smp).then_inc(ysm_out, 16)
            pool.wait_ge(ysm_out, 16)
            pool.dma_start(rows_sb[0][:, 0:D], scr_y).then_inc(ysm_back, 16)
            pool.wait_ge(state_ready, NCH)
            pool.dma_start(wkv_p_out, Pst).then_inc(wkv_sent, 16)
            pool.wait_ge(st_out, 64)
            pool.wait_ge(x_added, 2)
            pool.dma_start(arena[:, 0:2 * 2 * D + DC * KVL], mla_w).then_inc(mla_in, 16)
            pool.dma_start(cs.rearrange("p a b -> p (a b)"), rope.rearrange("p a b -> p (a b)")).then_inc(mla_in, 16)
            pool.wait_ge(kp_ready, 1)
            pool.dma_start(ckv_out, ckv).then_inc(lat_sent, 16)
            pool.dma_start(kpe_out, kp[0:ROPE, :]).then_inc(lat_sent, 16)
            pool.wait_ge(qp_ready, 1)

            def page(stream, at, dst, signal):
                phys = pool.value_load(ptab[0:1, bass.ds(at, 1)], min_val=0, max_val=POOL - 1)
                pool.dma_start(dst, stream[bass.ds(phys, 1), :, :].rearrange("o p n -> (o p) n")).then_inc(signal, 16)

            for n in range(4):
                page(cache_t, n, cpT[n].rearrange("p a b -> p (a b)"), page_in[n])
            with pool.Fori(1, PAGES // 4) as it:
                for n in range(4):
                    pool.wait_ge(page_used, it * 4 + (n - 3))
                    page(cache_t, it * 4 + n, cpT[n].rearrange("p a b -> p (a b)"), page_in[n])
            pool.wait_ge(nat_free, 1)
            for n in range(8):
                page(cache_n, n, cpN[n], natp_in[n])
            with pool.Fori(1, PAGES // 8) as it:
                for n in range(8):
                    pool.wait_ge(natp_used, it * 8 + (n - 7))
                    page(cache_n, it * 8 + n, cpN[n], natp_in[n])
            pool.wait_ge(x_added, 4)
            pool.dma_start(y_out, xbuf[:, :]).then_inc(y_sent, 16)
            pool.wait_ge(shift_sent, 16)
            pool.wait_ge(wkv_sent, 16)
            pool.wait_ge(lat_sent, 32)
            pool.wait_ge(y_sent, 16)


        @block.tensor
        def _(pe):
            w = Seen(pe)
            taken = [0] * 8

            def take(b, n=1):
                if taken[b]:
                    pe.wait_ge(bank_free[b], taken[b])
                taken[b] += n

            def tile(n):
                pe.wait_ge(slot_in[n % RING], 16 * (n // RING + 1))
                return slot(n)

            def mm(out, lhsT, rhs, start=True, stop=True, **kw):
                return nc.tensor.matmul(out, lhsT, rhs, start=start, stop=stop, **kw)

            def group_sums(src, n, lhsT):
                for i in range(n):
                    take(i)
                    mm(ps[:, i, 0:T], lhsT, src[:, i, :]).then_inc(for_dve, 1)

            def row_norm():
                w.next(sq_ready)
                take(0)
                for c in range(DC):
                    last = mm(ps[:, 0, 0:T], C("ones"), xn[:, c, :], c == 0, c == DC - 1)
                last.then_inc(for_dve, 1)

            def project(first, n, src, banks=(0, 1, 2, 3), kc=DC, rows=P):
                for o in range(n):
                    b = banks[o % len(banks)]
                    take(b)
                    wt = tile(first + o)
                    for c in range(kc):
                        last = mm(ps[0:rows, b, 0:T], wt[:, c, 0:rows], src[:, c, :], c == 0, c == kc - 1)
                    last.then_inc(tile_used, 1)

            def turn(out, src, rows=P):
                return nc.tensor.transpose(out, src, C("ident")[0:rows, 0:rows])

            def peer(layer):
                first = TILES[f"wq{layer}"]
                w.next(xn_ready)
                for g in range(16 + 1):
                    if g < 16:
                        take(g % 2)
                        wt = tile(first + g)
                        for c in range(DC):
                            last = mm(ps[:, g % 2, 0:T], wt[:, c, :], xn[:, c, :], c == 0, c == DC - 1)
                        last.then_inc(tile_used, 1)
                    if g >= 1:
                        w.next(q_copied)
                        take(2 + g % 2)
                        for i, (t0, nt) in enumerate(TT):
                            kc = (2 * layer + (g - 1) % 2) * P
                            last = mm(ps[0:nt, 2 + g % 2, i * P:(i + 1) * P], qb[(g - 1) % 2][:, t0:t0 + nt],
                                      skb[:, kc:kc + P])
                        last.then_inc(for_act, 1)
                for i, (t0, nt) in enumerate(TT):
                    w.next(sel_ready)
                    take(i)
                    for k in range(3):
                        last = turn(ps[:, i, k * P:k * P + nt], sel[0:nt, i, k, :], nt)
                    last.then_inc(for_dve, 1)
                oh0, gb0 = layer * (T // 2), [taken[b] for b in range(2)]
                marks[f"gates{layer}"] = list(taken)
                pe.sem_inc(oh_used, 2)
                with pe.Fori(0, T // 8) as it:
                    for b in range(2):
                        pe.wait_ge(bank_free[b], it + gb0[b])
                        for s in range(2):
                            pe.wait_ge(oh_ready, it * 4 + (oh0 + 2 * b + s + 1))
                            for u in range(2):
                                j = 2 * s + u
                                last = mm(ps[:, b, j * P:(j + 1) * P], hset[s][:, 0, u, :], hset[s][:, 1, u, :])
                            last.then_inc(oh_used, 1)
                for b in range(2):
                    taken[b] += T // 8
                t0 = TILES[f"peer{layer}"]
                base = [taken[b] for b in range(8)]
                marks[f"peer{layer}"] = base
                hr0 = layer * NGROUP

                def hidden(g, ut, it=0, par=None):
                    par = g % 2 if par is None else par
                    for u in range(GR):
                        b = 2 * par + u
                        pe.wait_ge(bank_free[b], base[b] + g // 2 + it)
                        n = ut + u
                        pe.wait_ge(slot_in[n % RING], 16 * (n // RING + 1) + it * 16)
                        for c in range(DC):
                            last = mm(ps[:, b, 0:T], slot(n)[:, c, :], xn[:, c, :], c == 0, c == DC - 1)
                        last.then_inc(tile_used, 1)

                def outputs(g, vt, it=0):
                    pe.wait_ge(h_ready, hr0 + g + 1 + it * 2)
                    for u in range(GR):
                        n = vt + u
                        pe.wait_ge(slot_in[n % RING], 16 * (n // RING + 1) + it * 16)
                    for c in range(DC):
                        b = 4 + c % 4
                        pe.wait_ge(bank_free[b], base[b] + 2 * g + c // 4 + it * 4)
                        for u in range(GR):
                            last = mm(ps[:, b, 0:T], slot(vt + u)[:, c, :], hg[:, g % 2 * GR + u, :],
                                      u == 0, u == GR - 1)
                            if c == DC - 1 and u == 0:
                                last.then_inc(tile_used, 1)
                        last.then_inc(tile_used if c == DC - 1 else for_dve, 1)

                hidden(0, t0)
                with pe.Fori(0, NGROUP // 2 - 1) as it:
                    hidden(1, t0 + 2, it)
                    outputs(0, t0 + 4, it)
                    hidden(2, t0 + 6, it)
                    outputs(1, t0 + 8, it)
                hidden(NGROUP - 1, t0 + 250)
                outputs(NGROUP - 2, t0 + 252)
                outputs(NGROUP - 1, t0 + 254)
                w.passed(h_ready, NGROUP)
                for b in range(4):
                    taken[b] += NGROUP // 2
                for b in range(4, 8):
                    taken[b] += 2 * NGROUP

            pe.wait_ge(consts_in, 16 * 7)
            row_norm()
            w.next(xn_ready)
            for m, name in enumerate(["r", "k", "v"]):
                w.next(mix_ready)
                project(TILES[name], 8, mix[m % 2])
            for m, (name, rows) in enumerate([("w1", 64), ("a1", 64), ("g1", 128)]):
                w.next(mix_ready)
                project(TILES[name], 1, mix[(3 + m) % 2], banks=(m,), rows=rows)
            for name, src, rows in [("w2", lw, 64), ("a2", la, 64), ("g2", lg, 128)]:
                w.next(lora_ready)
                wt = tile(TILES[name])
                for o in range(DC):
                    take(o % 4)
                    last = mm(ps[:, o % 4, 0:T], wt[0:rows, o, :], src[0:rows, :])
                    last.then_inc(tile_used if o == DC - 1 else for_act, 1)
            w.next(stat_ready)
            group_sums(tmp_t, DC, C("bd64"))
            w.next(stat_ready)
            group_sums(tmp_t, DC, C("bd64"))
            w.next(smp_ready)
            for j in range(6):
                for half in range(2):
                    b = (2 * j + half) % 4
                    take(b)
                    for c in range(4):
                        last = turn(ps[0:NS, b, c * P:(c + 1) * P], smp[:, j, half * 4 + c, :])
                    last.then_inc(for_act, 1)
            w.next(ops_ready)
            for c in range(DC):
                take(0)
                for i, src in enumerate([v_t, Kb]):
                    for j in range(2):
                        last = turn(ps[:, 0, (2 * i + j) * P:(2 * i + j + 1) * P], src[:, c, j * P:(j + 1) * P])
                last.then_inc(for_act, 1)
                take(1)
                for i, src in enumerate([Bb, kb]):
                    for j in range(2):
                        last = turn(ps[:, 1, (2 * i + j) * P:(2 * i + j + 1) * P], src[:, c, j * P:(j + 1) * P])
                last.then_inc(for_dve, 1)
                for bank0, moving in ((2, Kb), (4, Rb)):
                    for h in range(2):
                        take(bank0 + h)
                        pr = slice(64 * h, 64 * h + 64)
                        for i, stat in enumerate([Bb, kb]):
                            for j in range(2):
                                cols = slice(j * P, (j + 1) * P)
                                last = mm(ps[:, bank0 + h, (2 * i + j) * P:(2 * i + j + 1) * P],
                                          stat[pr, c, cols], moving[pr, c, cols])
                        last.then_inc(for_dve, 1)
                w.next(rows_act)
                w.next(ab_ready)
                take(6)
                for q in range(4):
                    last = mm(ps[:, 6, q * 64:(q + 1) * 64], q4(MTm)[:, q, :], Vrow[:, q % 2, q // 2, :])
                last.then_inc(for_act, 1)
                take(2)
                take(3)
                id4 = C("ident").unsqueeze(1).broadcast_to([P, 4, P])
                w.next(nt_ready)
                acc = dict(start=False, stop=True, skip_group_check=True)
                mm(ps[:, 2, :], C("ident"), id4, stop=True, skip_group_check=True)
                for q in range(4):
                    last = nc.tensor.matmul(ps[:, 2, q * P:(q + 1) * P], q4(NTl[0])[:, q, :], C("ident"), **acc)
                last.then_inc(for_act, 1)
                mm(ps[:, 3, :], C("ident"), id4, stop=True, skip_group_check=True)
                nc.tensor.matmul(ps[:, 3, :], C("ident"), NTl[0], **acc).then_inc(for_dve, 1)
                for lev in range(1, 6):
                    w.next(nt_ready)
                    w.next(x_ready)
                    take(7)
                    for q in range(4):
                        last = mm(ps[:, 7, q * P:(q + 1) * P], q4(NTl[lev % 2])[:, q, :], q4(Xs)[:, q, :])
                    last.then_inc(for_act, 1)
                    w.next(z_ready)
                    w.next(xt_ready)
                    for q in range(4):
                        last = nc.tensor.matmul(ps[:, 2, q * P:(q + 1) * P], q4(XTs)[:, q, :], q4(Zs)[:, q, :], **acc)
                    last.then_inc(for_act, 1)
                    for q in range(4):
                        last = nc.tensor.matmul(ps[:, 3, q * P:(q + 1) * P], q4(Zs)[:, q, :], q4(XTs)[:, q, :], **acc)
                    last.then_inc(for_dve, 1)
                w.next(xt_ready)
                w.next(rhs_ready)
                take(0)
                for q in range(4):
                    last = mm(ps[:, 0, q * P:(q + 1) * P], q4(XTs)[:, q, :], q4(RHS)[:, q, :])
                last.then_inc(for_act, 1)
                w.next(rows_dve)
                w.next(nwu_ready)
                take(1)
                take(4)
                take(5)
                take(6)
                for h in range(2):
                    pr = slice(64 * h, 64 * h + 64)
                    for j in range(2):
                        q = 2 * h + j
                        mm(ps[pr, 1, j * P:(j + 1) * P], q4(nWU)[:, q, 0:64], q4(ArbT)[:, q, :])
                        mm(ps[pr, 4, j * P:(j + 1) * P], Vrow[:, j, h, :], q4(ArkT)[:, q, :], True, False)
                        mm(ps[pr, 4, j * P:(j + 1) * P], q4(nWU)[:, q, 64:128], q4(ArbT)[:, q, :], False, True)
                BK = BKrow.rearrange("p (i j h k) -> p i j h k", i=2, j=2, h=2)
                for h in range(2):
                    pr = slice(64 * h, 64 * h + 64)
                    for j in range(2):
                        q = 2 * h + j
                        for half in range(2):
                            b, rw = 5 + half, slice(64 * half, 64 * half + 64)
                            mm(ps[pr, b, j * 64:(j + 1) * 64], q4(nWU)[rw, q, 0:64], BK[rw, 0, j, h, :])
                            o = ps[pr, b, 256 + j * 64:256 + (j + 1) * 64]
                            mm(o, BK[rw, 1, j, h, :], Vrow[rw, j, h, :], True, False)
                            last = mm(o, BK[rw, 0, j, h, :], q4(nWU)[rw, q, 64:128], False, True)
                last.then_inc(for_dve, 1)
                w.next(pair_done)
            for cc in range(1, NCH):
                w.next(state_ready)
                cols = slice(cc * 64, cc * 64 + 64)
                for kind in range(2):
                    for h in range(2):
                        b = 2 * kind + h
                        take(b)
                        pr = slice(64 * h, 64 * h + 64)
                        for c in range(DC):
                            if kind == 0:
                                last = mm(ps[pr, b, c * 64:(c + 1) * 64], Pst[pr, c, :], Rb[pr, c, cols])
                            else:
                                last = mm(ps[pr, b, c * 64:(c + 1) * 64], ETi[pr, c, cc, :], Pst[pr, c, :])
                        last.then_inc(for_dve, 1)
            w.next(ysm_back, 16)
            take(4)
            for c in range(DC):
                last = turn(ps[:, 4, c * NS:(c + 1) * NS], rows_sb[0][:, c * P:(c + 1) * P], NS)
            last.then_inc(for_dve, 1)
            w.next(stat_ready)
            group_sums(y_t, DC, C("bd64"))
            w.next(stat_ready)
            group_sums(tmp_t, DC, C("bd64"))
            w.next(yg_ready)
            project(TILES["rw_out"], 8, y_t)
            row_norm()
            peer(0)

            row_norm()
            w.next(xn_ready)
            project(TILES["mla_in"], 6, xn)
            w.next(sq_ready)
            take(0)
            for c in range(3):
                last = mm(ps[:, 0, 0:T], C("ones"), sqb[:, c, :], c == 0, c == 2)
            last.then_inc(for_dve, 1)
            take(1)
            for c in range(2):
                last = mm(ps[:, 1, 0:T], C("ones"), sqb[:, 3 + c, :], c == 0, c == 1)
            last.then_inc(for_dve, 1)
            take(2)
            mm(ps[:, 2, 0:T], C("bd32"), sqb[:, 5, :]).then_inc(for_dve, 1)
            w.next(lat_ready)
            take(3)
            mm(ps[:, 3, 0:T], C("rot"), kp).then_inc(for_dve, 1)
            w.next(mla_in, 32)
            project(TILES["qb"], 12, cq, kc=QC)
            for o in range(DC):
                take(o % 4)
                for c in range(2):
                    last = mm(ps[:, o % 4, 0:T], w_uk[:, c, o * P:(o + 1) * P], ckv[:, c, :], c == 0, c == 1)
                last.then_inc(for_act, 1)
            for j in range(2):
                for half in range(2):
                    b = 2 * j + half
                    take(b)
                    for c in range(2):
                        last = mm(ps[:, b, :], ckv[:, c, j * P:(j + 1) * P], w_uv[:, c, half * 512:(half + 1) * 512],
                                  c == 0, c == 1)
                    last.then_inc(for_act, 1)
            for n, mat in ((DC, "bd64"), (DC, "bd64"), (4, "bd32")):
                w.next(stat_ready)
                group_sums(sqb, n, C(mat))
            w.next(heads_ready)
            for i in range(4):
                take(i)
                mm(ps[:, i, 0:T], C("rot"), qr[:, i, :]).then_inc(for_dve, 1)
            w.next(heads_ready)
            for i in range(HEADS + 1):
                if i < HEADS:
                    s, c = i % 2, i // 2
                    w.next(qm_ready)
                    take(s)
                    for j in range(2):
                        o = ps[:, s, j * P:j * P + (j + 1) * P]
                        mm(o, qm[s][:, 0, j * P:(j + 1) * P], kn[:, c, 0:(j + 1) * P], True, False)
                        last = mm(o, qm[s][:, 1, j * P:(j + 1) * P], kp[:, 0:(j + 1) * P], False, True)
                    last.then_inc(for_dve, 1)
                if i >= 1:
                    h = i - 1
                    s = h % 2
                    w.next(p_ready)
                    take(2 + s)
                    for k in range(3):
                        last = turn(ps[:, 2 + s, k * P:(k + 1) * P], Sm[s][:, k * P:(k + 1) * P])
                    last.then_inc(for_act, 1)
                    w.next(pt_ready)
                    take(4 + s)
                    hv = slice(h * 64, h * 64 + 64)
                    mm(ps[:, 4 + s, 0:64], PTs[s][:, 0:P], vr[:, 0, hv])
                    mm(ps[:, 4 + s, 64:128], PTs[s][:, P:2 * P], vr[:, 0, hv], True, False)
                    mm(ps[:, 4 + s, 64:128], PTs[s][:, 2 * P:3 * P], vr[:, 1, hv], False, True).then_inc(for_dve, 1)
            w.next(o_ready)
            for j in range(2):
                for half in range(2):
                    b = 2 * j + half
                    take(b)
                    for c in range(4):
                        cc = half * 4 + c
                        last = turn(ps[:, b, c * P:(c + 1) * P], o_row[:, j, cc * P:(cc + 1) * P])
                    last.then_inc(for_act, 1)
            w.next(qs_ready)
            take(0)
            for cc in range(2):
                for c in range(DC):
                    o = cc * P + c * 16
                    last = mm(ps[:, 0, o:o + 16], w_ukT[:, c, cc * P:(cc + 1) * P],
                              qgm[:, c, :, :].rearrange("p h b -> p (h b)"))
            last.then_inc(for_dve, 1)
            take(1)
            for h in range(HEADS):
                o = ps[:, 1, h * NS:(h + 1) * NS]
                mm(o, C(f"half{h % 2}"), prodn[:, h // 2, :], True, False)
                last = mm(o, C(f"quar{h % 4}"), prodr[:, h // 4, :], False, True)
            last.then_inc(for_dve, 1)
            w.next(qp_ready)
            base = list(taken)
            marks["pages"] = base
            for b in (1, 3):
                pe.wait_ge(bank_free[b], taken[b])
            with pe.Fori(0, PAGES // 4) as it:
                for n in range(4):
                    pg = cpT[n]
                    b = 2 * (n % 2)
                    pe.wait_ge(page_in[n], it * 16 + 16)
                    pe.wait_ge(bank_free[b], it * 2 + (base[b] + n // 2))
                    for half in range(2):
                        for c in range(2):
                            last = mm(ps[:, b + half, :], pg[:, c, :], w_uk[:, c, half * 512:(half + 1) * 512],
                                      c == 0, c == 1)
                    last.then_inc(for_act, 1)
                    sbk = 4 + n % 2
                    pe.wait_ge(bank_free[sbk], it * 2 + (base[sbk] + n // 2))
                    req = it // 4
                    for c in range(2):
                        mm(ps[:, sbk, 0:16], pg[:, c, :], qp[:, c, bass.ds(req, 1), :].rearrange("p o h -> p (o h)"),
                           c == 0, c == 1)
                    mm(ps[:, sbk, 16:32], pg[:, 2, :], qrz[:, bass.ds(req, 1), :].rearrange("p o h -> p (o h)")
                       ).then_inc(page_used, 1)
            for b in (0, 2, 4, 5):
                taken[b] += PAGES // 2
            w.next(m1_ready)
            take(6)
            turn(ps[:, 6, 0:P], small[:, 0, :]).then_inc(for_dve, 1)
            w.next(dg_ready)
            take(7)
            mm(ps[:, 7, 0:P], C("ones"), small[:, 2, :]).then_inc(for_dve, 1)
            w.next(dg_ready)
            take(6)
            mm(ps[:, 6, 0:P], C("ones"), small[:, 5, :]).then_inc(for_dve, 1)
            base = list(taken)
            with pe.Fori(0, NS // 2) as it:
                for r in range(2):
                    pe.wait_ge(bank_free[r], it + base[r])
                    for p in range(NPAGE):
                        n = r * NPAGE + p
                        pe.wait_ge(natp_in[n % 8], it * 64 + 16 * (n // 8 + 1))
                        pe.wait_ge(bank_free[2 + r], it + base[2 + r]) if p == 0 else None
                        for c in range(2):
                            last = mm(ps[:, 2 * c + r, 0:16], cpN[n % 8][:, c * P:(c + 1) * P],
                                      PR[:, bass.ds(it * 2 * NPAGE + n, 1), :].rearrange("p o h -> p (o h)"),
                                      p == 0, p == NPAGE - 1)
                        last.then_inc(natp_used, 1)
            for b in range(4):
                taken[b] += NS // 2
            w.next(acc_ready)
            take(4)
            take(5)
            for h in range(HEADS):
                pr = slice(64 * (h % 2), 64 * (h % 2) + 64)
                o = ps[pr, 4 + h % 2, (h // 2) * NS:(h // 2 + 1) * NS]
                for c in range(2):
                    last = mm(o, w_uv[:, c, h * 64:(h + 1) * 64], accT[:, c, :, h], c == 0, c == 1)
            last.then_inc(for_dve, 1)
            w.next(oall_ready)
            project(TILES["mla_out"], 8, o_t)
            row_norm()
            peer(1)

        @block.scalar
        def _(act):
            w = Seen(act)
            steps = [0]

            def own(ins):
                steps[0] += 1
                ins.then_inc(act_step, 1)
                act.wait_ge(act_step, steps[0])

            def fn(out, in_, func=ACT.Copy, **kw):
                return nc.scalar.activation(out, in_, func, **kw)

            def tell(*sems):
                for s in sems:
                    act.sem_inc(s, 1)

            def row_norm():
                fn(xnbuf[:, :], xbuf[:, :], ACT.Square).then_inc(sq_ready, 1)
                root(rsb[:, 0:T])

            def root(x):
                w.next(rsq_in)
                fn(x, x, ACT.Sqrt).then_inc(rsq_out, 1)

            def peer(layer):
                w.next(x_added)
                row_norm()
                first = TILES[f"wq{layer}"]
                if layer == 0:
                    act.wait_ge(wkv_sent, 16)
                else:
                    act.wait_ge(lat_sent, 32)
                for g in range(17):
                    if g < 16:
                        act.wait_ge(tile_used, first + g + 1)
                        own(fn(qb[g % 2], ps[:, g % 2, 0:T]))
                        tell(q_copied, bank_free[g % 2])
                    if g >= 1:
                        w.next(for_act)
                        b = 2 + g % 2
                        own(fn(S[:, 0:2, g - 1, :], ps[:, b, 0:2 * P].rearrange("p (i n) -> p i n", i=2)))
                        own(fn(S[0:NS, 2, g - 1, :], ps[0:NS, b, 2 * P:3 * P]))
                        tell(bank_free[b])
                tell(s_copied)
                for i, (t0, nt) in enumerate(TT):
                    w.next(gate_in)
                    fn(ts16[0:nt], ts16[0:nt], ACT.Exp).then_inc(gate_exp, 1)
                oh0 = layer * (T // 2) + 2 * (layer + 1)
                with act.Fori(0, T // 8) as it:
                    for b in range(2):
                        act.wait_ge(oh_used, it * 4 + (oh0 + 2 * b + 2))
                        fn(G[:, :, bass.ds(it * 8 + 4 * b, 4)], ps[:, b, :].rearrange("p (t n) -> p n t", t=4)
                           ).then_inc(bank_free[b], 1)
                t0 = TILES[f"peer{layer}"]

                def gelu(g, ut, it=0):
                    for u in range(GR):
                        act.wait_ge(tile_used, ut + u + 1 + it * 8)
                        fn(hg[:, g % 2 * GR + u, :], ps[:, 2 * (g % 2) + u, 0:T], ACT.Gelu_apprx_tanh
                           ).then_inc(bank_free[2 * (g % 2) + u], 1)

                gelu(0, t0)
                with act.Fori(0, NGROUP // 2 - 1) as it:
                    gelu(1, t0 + 2, it)
                    gelu(2, t0 + 6, it)
                gelu(NGROUP - 1, t0 + 250)

            act.wait_ge(consts_in, 16 * 7)
            row_norm()
            for name, dst in (("r", r_t), ("k", k_t), ("v", v_t)):
                for o in range(DC):
                    act.wait_ge(tile_used, TILES[name] + o + 1)
                    fn(dst[:, o, :], ps[:, o % 4, 0:T]).then_inc(bank_free[o % 4], 1)
            for m, (name, dst, f, rows) in enumerate([("w1", lw, ACT.Tanh, 64), ("a1", la, ACT.Copy, 64),
                                                      ("g1", lg, ACT.Sigmoid, 128)]):
                act.wait_ge(tile_used, TILES[name] + 1)
                own(fn(dst[0:rows, :], ps[0:rows, m, 0:T], f))
                tell(lora_ready, bank_free[m])
            for name, dst in (("w2", ld_t), ("a2", a_t), ("g2", g_t)):
                for o in range(DC):
                    if o == DC - 1:
                        act.wait_ge(tile_used, TILES[name] + 1)
                    else:
                        w.next(for_act)
                    src = ps[:, o % 4, 0:T]
                    if name == "g2":
                        own(fn(dst[:, o, :], src))
                    else:
                        own(fn(dst[:, o, :], src, ACT.Sigmoid, bias=V("w0" if name == "w2" else "a0", o)))
                    tell(bank_free[o % 4])
            tell(proj_copied)
            w.next(ld_scaled)
            fn(smp[:, 5, :, :], ld_t[:, :, NP_:T], ACT.Exp).then_inc(smp_decay, 1)
            root(bon_t)
            for j in range(6):
                for half in range(2):
                    b = (2 * j + half) % 4
                    w.next(for_act)
                    own(fn(rows_sb[j // 2][:, (j % 2) * D + half * 512:(j % 2) * D + half * 512 + 512], ps[0:NS, b, :]))
                    tell(smp_rows, bank_free[b])
            act.wait_ge(smp_out, 48)
            w.next(cum_ready)
            fn(Rb, cum[1], ACT.Exp)
            fn(Kb, Kb, ACT.Exp)
            fn(Bb, cum[1], ACT.Exp, scale=-1.0).then_inc(e_ready, 1)
            for c in range(DC):
                w.next(for_act)
                rows = ps[:, 0, :].rearrange("p (i j h n) -> p i j h n", i=2, j=2, h=2)
                own(fn(Vrow, rows[:, 0]))
                own(fn(RHS.rearrange("p (h j n) -> p j h n", h=2, j=2)[:, :, :, 0:64], rows[:, 1]))
                tell(rows_act, bank_free[0])
                w.next(for_act)
                own(fn(q4(RHS)[:, :, 64:128], ps[:, 6, 0:256].rearrange("p (q n) -> p q n", q=4)))
                tell(rhs_ready, bank_free[6])
                w.next(for_act)
                fn(Xs, ps[:, 2, :]).then_inc(x_ready, 1)
                for lev in range(1, 6):
                    w.next(for_act)
                    own(fn(Zs, ps[:, 7, :]))
                    tell(z_ready, bank_free[7])
                    w.next(for_act)
                    if lev < 5:
                        fn(Xs, ps[:, 2, :]).then_inc(x_ready, 1)
                tell(bank_free[2])
                w.next(for_act)
                own(fn(nWU, ps[:, 0, :], ACT.Copy, scale=-1.0))
                tell(nwu_ready, bank_free[0])
            root(kk_t)
            act.wait_ge(shift_sent, 16)
            peer(0)

            w.next(x_added)
            row_norm()
            for o in range(6):
                act.wait_ge(tile_used, TILES["mla_in"] + o + 1)
                dst = cq[:, o, :] if o < 3 else ckv[:, o - 3, :] if o < 5 else kp
                own(fn(dst, ps[:, o % 4, 0:T]))
                tell(bank_free[o % 4])
            fn(sqb[:, 0:3, :], cq, ACT.Square)
            fn(sqb[:, 3:5, :], ckv, ACT.Square)
            fn(sqb[:, 5, :], kp, ACT.Square).then_inc(sq_ready, 1)
            root(rsb[:, :])
            for o in range(12):
                act.wait_ge(tile_used, TILES["qb"] + o + 1)
                own(fn(qn[:, o, :] if o < 8 else qr[:, o - 8, :], ps[:, o % 4, 0:T]))
                tell(bank_free[o % 4])
            for o in range(DC):
                w.next(for_act)
                own(fn(kn[:, o, :], ps[:, o % 4, 0:T]))
                tell(bank_free[o % 4])
            for j in range(2):
                for half in range(2):
                    w.next(for_act)
                    own(fn(vr[:, j, half * 512:(half + 1) * 512], ps[:, 2 * j + half, :]))
                    tell(bank_free[2 * j + half])
            tell(proj_copied)
            root(rs8)
            root(rs8)
            root(rs8[:, 0:4, :])
            for i in range(HEADS + 1):
                if i < HEADS:
                    s = i % 2
                    w.next(neg_ready)
                    fn(Sm[s][:, 0:P], Sm[s][:, 0:P], ACT.Exp, bias=mxl[s][:, 2:3], accum_out=mxl[s][:, 4:5])
                    own(fn(Sm[s][:, P:3 * P], Sm[s][:, P:3 * P], ACT.Exp, bias=mxl[s][:, 3:4],
                           accum_out=mxl[s][:, 5:6]))
                    tell(p_ready)
                if i >= 1:
                    s = (i - 1) % 2
                    w.next(for_act)
                    own(fn(PTs[s], ps[:, 2 + s, 0:3 * P]))
                    tell(pt_ready, bank_free[2 + s])
            for j in range(2):
                for half in range(2):
                    w.next(for_act)
                    own(fn(o_t[:, half * 4:half * 4 + 4, j * P:(j + 1) * P],
                           ps[:, 2 * j + half, :].rearrange("p (c n) -> p c n", c=4)))
                    tell(bank_free[2 * j + half])
            tell(oT_copied)
            fa = w.count(for_act)
            with act.Fori(0, PAGES // 4) as it:
                for n in range(4):
                    b = 2 * (n % 2)
                    act.wait_ge(for_act, it * 4 + (fa + n + 1))
                    act.wait_ge(sqp_used, it * 4 + (n + 1))
                    fn(sqp[n % 2].rearrange("p (a n) -> p a n", a=2), ps[:, b:b + 2, :], ACT.Square
                       ).then_inc(bank_free[b], 1)
            w.passed(for_act, PAGES)
            root(SS)
            w.next(pr_in)
            fn(PR, PR, ACT.Exp)
            fn(small[:, 3, :], small[:, 3, :], ACT.Exp).then_inc(pr_exp, 1)
            peer(1)

        @block.vector
        def _(dve):
            w = Seen(dve)
            v = nc.vector
            steps = [0]

            def own(ins):
                steps[0] += 1
                ins.then_inc(dve_step, 1)
                dve.wait_ge(dve_step, steps[0])

            def tell(*sems):
                for s in sems:
                    dve.sem_inc(s, 1)

            def tt(out, a, b, op):
                return v.tensor_tensor(out, a, b, op)

            def root(x):
                v.reciprocal(x, x).then_inc(rsq_in, 1)
                w.next(rsq_out)

            def row_norm(gain):
                rs = rsb[:, 0:T]
                w.next(for_dve)
                own(v.tensor_scalar(rs, ps[:, 0, 0:T], 1.0 / D, EPS, ALU.mult, ALU.add))
                tell(bank_free[0])
                root(rs)
                for c in range(DC):
                    last = v.scalar_tensor_tensor(xn[:, c, :], xT[:, c, :], V(gain, c), rs, ALU.mult, ALU.mult)
                last.then_inc(xn_ready, 1)
                w.next(xn_ready)

            def take_sums(n, op):
                for i in range(n):
                    w.next(for_dve)
                    own(op(i))
                    tell(bank_free[i])

            def residual(first):
                for o in range(DC):
                    dve.wait_ge(tile_used, first + o + 1)
                    own(tt(xT[:, o, :], ps[:, o % 4, 0:T], xT[:, o, :], ALU.add))
                    tell(bank_free[o % 4])
                tell(x_added)

            def top16(vals, places, src, work, groups):
                for g in groups:
                    last = v.max(vals[:, g, 0:8], src[:, g, :])
                own(last)
                for g in groups:
                    v.max_index(places[:, g, 0:8], vals[:, g, 0:8], src[:, g, :])
                    last = v.match_replace(work[:, g, :], vals[:, g, 0:8], src[:, g, :], VERY_NEG)
                own(last)
                for g in groups:
                    last = v.max(vals[:, g, 8:16], work[:, g, :])
                own(last)
                for g in groups:
                    last = v.max_index(places[:, g, 8:16], vals[:, g, 8:16], work[:, g, :])
                own(last)

            def choose(i, nt):
                top16(v16[0:nt], i16u[0:nt], S[0:nt, i], S2[0:nt], range(16))
                own(v.tensor_copy(i16f[0:nt], i16u[0:nt]))
                hv = v16[0:nt].rearrange("p (h two) k -> p h two k", two=2)
                hi = i16f[0:nt].rearrange("p (h two) k -> p h two k", two=2)
                shape = [nt, PH, TOPK, TOPK]
                c4 = cand[0:nt].rearrange("p h (a b) -> p h a b", a=TOPK)
                own(tt(c4, hv[:, :, 0, :].unsqueeze(3).broadcast_to(shape),
                       hv[:, :, 1, :].unsqueeze(2).broadcast_to(shape), ALU.add))
                top16(ts16[0:nt], posu[0:nt], cand[0:nt], cand2[0:nt], range(PH))
                own(v.tensor_copy(smax[0:nt], ts16[0:nt, :, 0:1]))
                tt(ts16[0:nt], ts16[0:nt], smax[0:nt].broadcast_to([nt, PH, TOPK]), ALU.subtract
                   ).then_inc(gate_in, 1)
                pos = posu[0:nt].rearrange("p h k -> p (h k)")
                v.tensor_scalar(abu[0:nt, 0, :], pos, 4, None, ALU.logical_shift_right)
                own(v.tensor_scalar(abu[0:nt, 1, :], pos, 15, None, ALU.bitwise_and))
                own(v.tensor_copy(abf[0:nt], abu[0:nt]))
                for k in range(2):
                    e3 = eq[0:nt].rearrange("p h (a b) -> p (h a) b", a=TOPK)
                    e4 = eq[0:nt].rearrange("p h (a b) -> p h a b", a=TOPK)
                    own(tt(e3, abf[0:nt, k, :].unsqueeze(2).broadcast_to([nt, P, TOPK]),
                           C("iota")[0:nt, 0:TOPK].unsqueeze(1).broadcast_to([nt, P, TOPK]), ALU.is_equal))
                    own(tt(e4, e4, hi[:, :, k, :].unsqueeze(2).broadcast_to(shape), ALU.mult))
                    own(v.tensor_reduce(sel[0:nt, i, k, :], e3, AX.X, ALU.add))
                w.next(gate_exp)
                own(v.tensor_reduce(smax[0:nt].rearrange("p h o -> p (h o)"), ts16[0:nt], AX.X, ALU.add))
                own(v.reciprocal(smax[0:nt], smax[0:nt]))
                tt(sel[0:nt, i, 2, :].rearrange("p (h k) -> p h k", h=PH), ts16[0:nt],
                   smax[0:nt].broadcast_to([nt, PH, TOPK]), ALU.mult).then_inc(sel_ready, 1)
                w.next(sel_ready)

            def peer(layer):
                row_norm(f"norm_ffn{layer}")
                w.next(s_copied)
                for i, (t0_, nt) in enumerate(TT):
                    choose(i, nt)
                for i, (t0_, nt) in enumerate(TT):
                    w.next(for_dve)
                    own(v.tensor_copy(idx[:, :, t0_:t0_ + nt],
                                      ps[:, i, 0:3 * P].rearrange("p (k n) -> p k n", k=3)[:, :, 0:nt]))
                    tell(bank_free[i])
                m0 = layer * (T // 2) + 2 * layer + 1
                with dve.Fori(0, T // 8) as it:
                    for k in range(4):
                        hs = hset[k % 2]
                        dve.wait_ge(oh_used, it * 4 + (m0 + k))
                        for u in range(2):
                            t = it * 8 + (2 * k + u)
                            v.tensor_scalar(hs[:, 0, u, :], C("iota"), idx[:, 0, bass.ds(t, 1)], None, ALU.is_equal)
                            last = v.tensor_scalar(hs[:, 1, u, :], C("iota"), idx[:, 1, bass.ds(t, 1)],
                                                   idx[:, 2, bass.ds(t, 1)], ALU.is_equal, ALU.mult)
                        last.then_inc(oh_ready, 1)
                base = marks[f"peer{layer}"]
                for b in range(2):
                    dve.wait_ge(bank_free[b], base[b])
                t0 = TILES[f"peer{layer}"]
                fd = w.count(for_dve)

                def gate(g, it=0):
                    for u in range(GR):
                        b = 2 * (g % 2) + u
                        dve.wait_ge(bank_free[b], base[b] + g // 2 + 1 + it)
                        hgu = hg[:, g % 2 * GR + u, :]
                        last = tt(hgu, hgu, G[:, bass.ds(it * (2 * GR) + (g * GR + u), 1), :].rearrange("p o t -> p (o t)"),
                                  ALU.mult)
                    last.then_inc(h_ready, 1)

                def add(g, vt, it=0):
                    for c in range(DC):
                        if c == DC - 1:
                            dve.wait_ge(tile_used, vt + 2 + it * 8)
                        else:
                            dve.wait_ge(for_dve, fd + 7 * g + c + 1 + it * 14)
                        tt(xT[:, c, :], ps[:, 4 + c % 4, 0:T], xT[:, c, :], ALU.add).then_inc(bank_free[4 + c % 4], 1)

                gate(0)
                with dve.Fori(0, NGROUP // 2 - 1) as it:
                    gate(1, it)
                    add(0, t0 + 4, it)
                    gate(2, it)
                    add(1, t0 + 8, it)
                gate(NGROUP - 1)
                add(NGROUP - 2, t0 + 252)
                add(NGROUP - 1, t0 + 254)
                w.passed(for_dve, 7 * NGROUP)
                dve.wait_ge(bank_free[7], base[7] + 2 * NGROUP)
                tell(x_added)

            def sample_quarter(qd):
                st = st_q[qd % 2]
                rr, kr, vr_, kkr, br, dr = (smp_row[:, j, :] for j in range(6))
                row = lambda x: x.unsqueeze(1).broadcast_to([P, 16, 64])
                col = lambda x: x.unsqueeze(2).broadcast_to([P, 16, 64])
                dve.wait_ge(st_in[qd % 2], 16 * (qd // 2 + 1))
                own(tt(st_tmp, st, row(kkr), ALU.mult))
                own(v.tensor_reduce(skk, st_tmp, AX.X, ALU.add))
                own(tt(st, st, row(dr), ALU.mult))
                own(tt(st_tmp, col(skk), row(br), ALU.mult))
                own(tt(st, st, st_tmp, ALU.subtract))
                own(tt(st_tmp, col(vr_[:, 16 * qd:16 * qd + 16]), row(kr), ALU.mult))
                own(tt(st, st, st_tmp, ALU.add))
                own(tt(st_tmp, st, row(rr), ALU.mult))
                v.tensor_reduce(y_smp[:, 16 * qd:16 * qd + 16], st_tmp, AX.X, ALU.add).then_inc(st_done, 1)
                w.next(st_done)

            dve.wait_ge(consts_in, 16 * 7)
            row_norm("norm_mix0")
            tt(xx[:, :, 1:NP_], xn[:, :, 0:NP_ - 1], xn[:, :, 1:NP_], ALU.subtract)
            v.tensor_scalar(xx[:, :, 0:1], xn[:, :, 0:1], -1.0, None, ALU.mult)
            own(tt(xx[:, :, NP_:T], shift_sb, xn[:, :, NP_:T], ALU.subtract))
            users = [TILES["r"] + 8, TILES["k"] + 8, TILES["v"] + 8, TILES["w1"] + 1, TILES["a1"] + 1]
            for m, mu in enumerate([0, 2, 3, 1, 4, 5]):
                if m >= 2:
                    dve.wait_ge(tile_used, users[m - 2])
                for c in range(DC):
                    last = v.scalar_tensor_tensor(mix[m % 2][:, c, :], xx[:, c, :], V(f"mu{mu}", c), xn[:, c, :],
                                                  ALU.mult, ALU.add)
                last.then_inc(mix_ready, 1)
            w.next(proj_copied)
            v.tensor_scalar(ld_t, ld_t, -float(np.exp(-0.5)), None, ALU.mult).then_inc(ld_scaled, 1)
            own(tt(kk_t, k_t, vb("k_k"), ALU.mult))
            tt(tmp_t, kk_t, kk_t, ALU.mult).then_inc(stat_ready, 1)
            own(v.scalar_tensor_tensor(bon_t, a_t, -1.0, vb("k_a"), ALU.add, ALU.mult))
            own(v.scalar_tensor_tensor(k_t, bon_t, 1.0, k_t, ALU.add, ALU.mult))
            take_sums(DC, lambda i: v.tensor_scalar(bon_t[:, i, :], ps[:, i, 0:T], 1e-24, None, ALU.max))
            root(bon_t)
            own(tt(kk_t, kk_t, bon_t, ALU.mult))
            own(tt(a_t, a_t, kk_t, ALU.mult))
            own(tt(tmp_t, r_t, k_t, ALU.mult))
            tt(tmp_t, tmp_t, vb("r_k"), ALU.mult).then_inc(stat_ready, 1)
            for j, src in enumerate([r_t, k_t, v_t, kk_t, a_t]):
                last = v.tensor_copy(smp[:, j, :, :], src[:, :, NP_:T])
            own(last)
            w.next(smp_decay)
            tell(smp_ready)
            src = ld_t[:, :, 0:NP_]
            for lev in range(6):
                n = 1 << lev
                dst = cum[lev % 2]
                s4 = src.rearrange("p c (g t) -> p c g t", t=CH)
                d4 = dst.rearrange("p c (g t) -> p c g t", t=CH)
                v.tensor_copy(d4[:, :, :, 0:n], s4[:, :, :, 0:n])
                own(tt(d4[:, :, :, n:CH], s4[:, :, :, n:CH], s4[:, :, :, 0:CH - n], ALU.add))
                src = dst
            take_sums(DC, lambda i: tt(bon_t[:, i, :], ps[:, i, 0:T], v_t[:, i, :], ALU.mult))
            tt(Kb, cum[1], ld_t[:, :, 0:NP_], ALU.subtract).then_inc(cum_ready, 1)
            w.next(e_ready)
            own(v.tensor_copy(lam, Rb.rearrange("p c (g t) -> p c g t", t=CH)[:, :, :, CH - 1]))
            tt(Rb, Rb, r_t[:, :, 0:NP_], ALU.mult)
            tt(Kb, Kb, kk_t[:, :, 0:NP_], ALU.mult)
            own(tt(kb, Bb, k_t[:, :, 0:NP_], ALU.mult))
            tt(Bb, Bb, a_t[:, :, 0:NP_], ALU.mult).then_inc(ops_ready, 1)
            w.next(ops_ready)
            dve.wait_ge(smp_back, 16 * 6)

            def mask(m):
                return wm[:, m, :].unsqueeze(1).broadcast_to([P, 4, P])

            def mask2(m):
                return wm[:, m, :].unsqueeze(1).unsqueeze(1).broadcast_to([P, 2, 2, P])

            for c in range(DC):
                w.next(for_dve)
                own(v.tensor_copy(BKrow, ps[:, 1, :]))
                tell(rows_dve, bank_free[1])
                w.next(for_dve, 2)
                two = lambda x: x.rearrange("p (h n) -> p h n", h=2)
                own(v.tensor_copy(two(LT), ps[:, 2:4, 0:256]))
                hj = lambda x: x.rearrange("p (h j n) -> p h j n", h=2, j=2)
                hp = lambda x: x.rearrange("p h (j n) -> p h j n", j=2)
                tt(q4(NTl[0]), q4(LT), mask(2), ALU.mult).then_inc(nt_ready, 1)
                own(tt(hj(MTm), hp(ps[:, 2:4, 256:512]), mask2(0), ALU.mult))
                tell(bank_free[2], bank_free[3])
                tt(q4(NTl[1]), q4(LT), mask(3), ALU.mult).then_inc(nt_ready, 1)
                w.next(for_dve, 2)
                own(tt(hj(ArbT), hp(ps[:, 4:6, 0:256]), mask2(1), ALU.mult))
                own(tt(hj(ArkT), hp(ps[:, 4:6, 256:512]), mask2(1), ALU.mult))
                tell(ab_ready, bank_free[4], bank_free[5])
                for lev in range(6):
                    w.next(for_dve)
                    own(v.tensor_copy(XTs, ps[:, 3, :]))
                    tell(xt_ready)
                    if lev + 2 < 6:
                        tt(q4(NTl[lev % 2]), q4(LT), mask(2 + lev + 2), ALU.mult).then_inc(nt_ready, 1)
                tell(bank_free[3])
                if c % 2 == 1:
                    sample_quarter(c // 2)
                w.next(for_dve)
                own(tt(Rb[:, c, :], ps[:, 1, 0:NP_], Rb[:, c, :], ALU.add))
                own(v.tensor_copy(y_t[:, c, 0:NP_], ps[:, 4, 0:NP_]))
                for half in range(2):
                    pick = lambda x: x.rearrange("p (j f) k -> p j f k", f=2)[:, :, half, :]
                    own(tt(pick(ETi[:, c]), ps[:, 5 + half, 0:P].rearrange("p (j k) -> p j k", j=2),
                           C("stack")[:, 0:64].unsqueeze(1).broadcast_to([P, 2, 64]), ALU.add))
                    own(v.tensor_copy(pick(Hk[:, c]), ps[:, 5 + half, 256:256 + P].rearrange("p (j k) -> p j k", j=2)))
                tell(bank_free[1], bank_free[4], bank_free[5], bank_free[6], pair_done)
            lamb = lambda cc, rows=slice(0, P): lam[rows, :, cc].unsqueeze(2).broadcast_to([rows.stop - rows.start, DC, 64])
            tt(Pst, Hk[:, :, 0, :], lamb(0), ALU.mult).then_inc(state_ready, 1)
            w.next(state_ready)
            for cc in range(1, NCH):
                cols = slice(cc * 64, cc * 64 + 64)
                for h in range(2):
                    w.next(for_dve)
                    pr = slice(64 * h, 64 * h + 64)
                    own(tt(y_t[pr, :, cols], ps[pr, h, :].rearrange("p (c v) -> p c v", c=DC), y_t[pr, :, cols], ALU.add))
                    tell(bank_free[h])
                w.next(for_dve, 2)
                for h in range(2):
                    pr = slice(64 * h, 64 * h + 64)
                    own(tt(Pst[pr], ps[pr, 2 + h, :].rearrange("p (c v) -> p c v", c=DC), Hk[pr, :, cc, :], ALU.add))
                    tell(bank_free[2 + h])
                tt(Pst, Pst, lamb(cc), ALU.mult).then_inc(state_ready, 1)
                w.next(state_ready)
            w.next(for_dve)
            own(v.tensor_copy(y_t[:, :, NP_:T], ps[:, 4, 0:DC * NS].rearrange("p (c b) -> p c b", c=DC)))
            tell(bank_free[4], stat_ready)
            take_sums(DC, lambda i: v.scalar_tensor_tensor(y_t[:, i, :], ps[:, i, 0:T], -1.0 / 64, y_t[:, i, :],
                                                           ALU.mult, ALU.add))
            tt(tmp_t, y_t, y_t, ALU.mult).then_inc(stat_ready, 1)
            take_sums(DC, lambda i: v.tensor_scalar(kk_t[:, i, :], ps[:, i, 0:T], 1.0 / 64, GN_EPS, ALU.mult, ALU.add))
            root(kk_t)
            own(tt(y_t, y_t, kk_t, ALU.mult))
            for c in range(DC):
                last = v.tensor_scalar(y_t[:, c, :], y_t[:, c, :], V("ln_w", c), V("ln_b", c), ALU.mult, ALU.add)
            own(last)
            own(tt(y_t, y_t, bon_t, ALU.add))
            tt(y_t, y_t, g_t, ALU.mult).then_inc(yg_ready, 1)
            residual(TILES["rw_out"])
            peer(0)

            row_norm("norm_mix1")
            for i, n in enumerate((QL, KVL, ROPE)):
                w.next(for_dve)
                own(v.tensor_scalar(rsb[:, i * T:(i + 1) * T], ps[:, i, 0:T], 1.0 / n, EPS, ALU.mult, ALU.add))
                tell(bank_free[i])
            root(rsb[:, :])
            for c in range(3):
                v.scalar_tensor_tensor(cq[:, c, :], cq[:, c, :], V("q_norm", c), rsb[:, 0:T], ALU.mult, ALU.mult)
            for c in range(2):
                v.scalar_tensor_tensor(ckv[:, c, :], ckv[:, c, :], V("kv_norm", c), rsb[:, T:2 * T], ALU.mult, ALU.mult)
            own(v.scalar_tensor_tensor(kp, kp, V("kn_rope"), rsb[:, 2 * T:3 * T], ALU.mult, ALU.mult))
            tell(lat_ready)
            dve.wait_ge(mla_in, 32)
            w.next(for_dve)
            own(tt(sqb[:, 0, :], ps[:, 3, 0:T], cs[:, 1, :], ALU.mult))
            tell(bank_free[3])
            own(tt(kp, kp, cs[:, 0, :], ALU.mult))
            own(tt(kp, kp, sqb[:, 0, :], ALU.add))
            tell(kp_ready)
            w.next(proj_copied)
            for x, n, gain, size in ((qn, DC, "qn_nope", 64), (kn, DC, "kn_nope", 64), (qr, 4, "qn_rope", 32)):
                tt(sqb[:, 0:n, :], x, x, ALU.mult).then_inc(stat_ready, 1)
                take_sums(n, lambda i: v.tensor_scalar(rs8[:, i, :], ps[:, i, 0:T], 1.0 / size, EPS, ALU.mult, ALU.add))
                root(rs8[:, 0:n, :])
                own(v.scalar_tensor_tensor(x, x, V(gain), rs8[:, 0:n, :], ALU.mult, ALU.mult))
            tell(heads_ready)
            both = lambda x: x.unsqueeze(1).broadcast_to([P, 4, T])
            take_sums(4, lambda i: tt(sqb[:, i, :], ps[:, i, 0:T], cs[:, 1, :], ALU.mult))
            own(tt(qr, qr, both(cs[:, 0, :]), ALU.mult))
            own(tt(qr, qr, sqb[:, 0:4, :], ALU.add))
            tell(heads_ready, nat_free)

            def masked_query(h):
                s = h % 2
                v.tensor_scalar(qm[s][:, 0, :], qn[:, h // 2, 0:NP_], C(f"half{h % 2}", 1), None, ALU.mult)
                v.tensor_scalar(qm[s][:, 1, :], qr[:, h // 4, 0:NP_], C(f"quar{h % 4}", 1), None, ALU.mult
                                ).then_inc(qm_ready, 1)

            masked_query(0)
            for i in range(HEADS + 1):
                if i < HEADS:
                    if i + 1 < HEADS:
                        masked_query(i + 1)
                    s = i % 2
                    w.next(for_dve)
                    own(v.scalar_tensor_tensor(Sm[s], ps[:, s, 0:3 * P], SCALE, C("amask", 3 * P), ALU.mult, ALU.add))
                    tell(bank_free[s])
                    v.tensor_reduce(mxl[s][:, 0:1], Sm[s][:, 0:P], AX.X, ALU.max)
                    own(v.tensor_reduce(mxl[s][:, 1:2], Sm[s][:, P:3 * P], AX.X, ALU.max))
                    v.tensor_scalar(mxl[s][:, 2:4], mxl[s][:, 0:2], -1.0, None, ALU.mult).then_inc(neg_ready, 1)
                if i >= 1:
                    h, s = i - 1, (i - 1) % 2
                    w.next(for_dve)
                    own(v.reciprocal(mxl[s][:, 6:8], mxl[s][:, 4:6]))
                    for j in range(2):
                        own(v.tensor_scalar(o_row[:, j, h * 64:(h + 1) * 64], ps[:, 4 + s, j * 64:(j + 1) * 64],
                                            mxl[s][:, 6 + j:7 + j], None, ALU.mult))
                    tell(bank_free[4 + s])
            tell(o_ready)
            qs, ks, rs_, kps = qn[:, :, NP_:T], kn[:, :, NP_:T], qr[:, :, NP_:T], kp[:, NP_:T]
            tt(prodn, qs, ks, ALU.mult)
            tt(prodr, rs_, kps.unsqueeze(1).broadcast_to([P, 4, NS]), ALU.mult)
            for h in range(2):
                v.tensor_scalar(qgm[:, :, h, :], qs, V("kn_nope"), C(f"half{h}", 1), ALU.mult, ALU.mult)
            for m in range(4):
                last = v.tensor_scalar(qrz.rearrange("p b (g m) -> p m g b", m=4)[:, m], rs_, C(f"quar{m}", 1), None,
                                       ALU.mult)
            own(last)
            tell(qs_ready)
            w.next(for_dve)
            for c in range(2):
                own(v.tensor_copy(qp[:, c].rearrange("p b h -> p h b"),
                                  ps[:, 0, c * P:(c + 1) * P].rearrange("p (h b) -> p h b", h=HEADS)))
            w.next(for_dve)
            own(v.tensor_scalar(small[:, 3, :].rearrange("p (b h) -> p h b", h=HEADS),
                                ps[:, 1, 0:P].rearrange("p (h b) -> p h b", h=HEADS), SCALE, None, ALU.mult))
            tell(bank_free[0], bank_free[1], qp_ready)
            dve.sem_inc(sqp_used, 2)
            base = marks["pages"]
            with dve.Fori(0, PAGES // 4) as it:
                for n in range(4):
                    b = 2 * (n % 2)
                    at = it * 4 + n
                    dve.wait_ge(bank_free[b], it * 2 + (base[b] + n // 2 + 1))
                    v.tensor_reduce(SS[:, bass.ds(at, 1), :].rearrange("p o h -> p (o h)"),
                                    sqp[n % 2].rearrange("p (h d) -> p h d", h=HEADS), AX.X, ALU.add).then_inc(sqp_used, 1)
                    dve.wait_ge(page_used, it * 4 + (n + 1))
                    v.tensor_copy(SN[:, bass.ds(at, 1), :].rearrange("p o h -> p (o h)"), ps[:, 4 + n % 2, 0:32]
                                  ).then_inc(bank_free[4 + n % 2], 1)
            dve.wait_ge(bank_free[5], base[5] + PAGES // 2)
            own(v.tensor_scalar(SS, SS, 1.0 / 64, EPS, ALU.mult, ALU.add))
            root(SS)
            own(v.scalar_tensor_tensor(PR, SN[:, :, 0:16], SCALE, SS, ALU.mult, ALU.mult))
            own(v.scalar_tensor_tensor(PR, SN[:, :, 16:32], SCALE, PR, ALU.mult, ALU.add))
            by_req = lambda x: x.rearrange("p (b g) h -> p b h g", b=NS)
            bh = lambda i: small[:, i, :].rearrange("p (b h) -> p b h", b=NS)
            own(v.tensor_reduce(bh(0), by_req(PR), AX.X, ALU.max))
            tell(m1_ready)
            w.next(for_dve)
            own(v.tensor_reduce(small[:, 1, 0:1], ps[:, 6, 0:P], AX.X, ALU.max))
            own(v.tensor_scalar(small[:, 2, :], C("ident"), small[:, 1, 0:1], None, ALU.mult))
            tell(bank_free[6], dg_ready)
            w.next(for_dve)
            own(tt(small[:, 4, :], ps[:, 7, 0:P], small[:, 3, :], ALU.max))
            tell(bank_free[7])
            PR4 = PR.rearrange("p (b g) h -> p b g h", b=NS)
            tt(PR4, PR4, bh(4).unsqueeze(2).broadcast_to([P, NS, NPAGE, HEADS]), ALU.subtract)
            own(tt(small[:, 3, :], small[:, 3, :], small[:, 4, :], ALU.subtract))
            tell(pr_in)
            w.next(pr_exp)
            own(v.tensor_reduce(bh(5), by_req(PR), AX.X, ALU.add))
            tell(dg_ready)
            w.next(for_dve)
            own(tt(small[:, 6, :], ps[:, 6, 0:P], small[:, 3, :], ALU.add))
            tell(bank_free[6])
            own(v.reciprocal(small[:, 6, :], small[:, 6, :]))
            with dve.Fori(0, NS // 2) as it:
                for r in range(2):
                    dve.wait_ge(natp_used, it * 32 + 16 * (r + 1))
                    for c in range(2):
                        v.tensor_copy(accT[:, c, bass.ds(it * 2 + r, 1), :].rearrange("p o h -> p (o h)"),
                                      ps[:, 2 * c + r, 0:16]).then_inc(bank_free[2 * c + r], 1)
            new = ckv[:, :, NP_:T].unsqueeze(3).broadcast_to([P, 2, NS, HEADS])
            for c in range(2):
                own(tt(cnew[:, c], new[:, c], bh(3), ALU.mult))
                own(tt(accT[:, c], accT[:, c], cnew[:, c], ALU.add))
                own(tt(accT[:, c], accT[:, c], bh(6), ALU.mult))
            tell(acc_ready)
            w.next(for_dve)
            for h in range(2):
                pr = slice(64 * h, 64 * h + 64)
                own(v.tensor_copy(o_t[pr, :, NP_:T], ps[pr, 4 + h, 0:DC * NS].rearrange("p (c b) -> p c b", c=DC)))
            tell(bank_free[4], bank_free[5])
            w.next(oT_copied)
            tell(oall_ready)
            residual(TILES["mla_out"])
            peer(1)


def kernel(**inputs):
    import concourse.bacc as _bacc
    from concourse.bass_utils import run_bass_kernel_spmd as _run

    f = {k: np.asarray(a) for k, a in inputs.items()}
    con = np.ascontiguousarray

    def chunks(x):
        return con(x.T.reshape(DC, P, -1).transpose(1, 0, 2))

    def tiles(wt, cols=P):
        k, m = wt.shape
        out = np.zeros((m // cols, P, DC, P), np.float32)
        out[:, :, :k // P, :cols] = wt.reshape(k // P, P, m // cols, cols).transpose(2, 1, 0, 3)
        return out.reshape(-1, P, D)

    def hidden_rows(wt):
        out = np.zeros((1, P, D), np.float32)
        out[0, :wt.shape[0]] = wt
        return out

    def experts(u, vt):
        ut = u.reshape(P, P, DC, P).transpose(1, 3, 2, 0).reshape(P, P, D)
        vt = vt.reshape(P, P, D).transpose(1, 0, 2)
        out = [ut[0:GR]]
        for g in range(1, NGROUP):
            out += [ut[GR * g:GR * g + GR], vt[GR * (g - 1):GR * g]]
        return out + [vt[P - GR:]]

    x_t = chunks(np.concatenate([f["x_prompt"][0], f["x_sample"][:, 0]], 0))
    shift_t = chunks(f["state_shift"][0])
    vs = {"norm_mix0": f["norm_mix"][0], "norm_mix1": f["norm_mix"][1], "norm_ffn0": f["norm_ffn"][0],
          "norm_ffn1": f["norm_ffn"][1], "w0": f["rw_w0"], "a0": f["rw_a0"], "k_k": f["rw_k_k"], "k_a": f["rw_k_a"],
          "r_k": f["rw_r_k"], "ln_w": f["rw_ln_w"], "ln_b": f["rw_ln_b"]}
    for m in range(6):
        vs[f"mu{m}"] = f["rw_mu"][0, m]
    vecs = [vs[n].reshape(DC, P).T for n in VECS]
    vecs += [f["mla_q_norm"].reshape(3, P).T, f["mla_kv_norm"].reshape(2, P).T]
    for n, rep in (("mla_qn_nope", 2), ("mla_qn_rope", 4), ("mla_kn_nope", 2), ("mla_kn_rope", 4)):
        vecs.append(np.tile(f[n][0], rep)[:, None])
    vecs = con(np.concatenate(vecs, 1))
    consts, wmasks, rope = const_arrays()

    w_in = f["mla_w_in"][0]
    w_in = np.concatenate([w_in[:, :QL + KVL], np.tile(w_in[:, QL + KVL:], (1, 4))], 1)
    w_qb = f["mla_w_qb"][0].reshape(QL, HEADS, 96)
    w_qb = np.concatenate([w_qb[:, :, :64].reshape(QL, D), w_qb[:, :, 64:].reshape(QL, 512)], 1)
    parts = [tiles(f["rw_w_in"][0, m]) for m in range(3)]
    parts += [tiles(f["rw_w1"][0], 64), tiles(f["rw_a1"][0], 64), tiles(f["rw_g1"][0])]
    parts += [hidden_rows(f["rw_w2"][0]), hidden_rows(f["rw_a2"][0]), hidden_rows(f["rw_g2"][0])]
    parts += [tiles(f["rw_w_out"][0]), tiles(f["peer_w_q"][0])] + experts(f["peer_u"][0], f["peer_v"][0])
    parts += [tiles(w_in), tiles(w_qb), tiles(f["mla_w_out"][0]), tiles(f["peer_w_q"][1])]
    parts += experts(f["peer_u"][1], f["peer_v"][1])
    wstream = np.concatenate(parts, 0)
    assert wstream.shape[0] == NTILES

    sub_keys = con(f["peer_sub_keys"].transpose(3, 0, 1, 2).reshape(P, 4 * P))
    kvb = f["mla_w_kvb"][0].reshape(KVL, HEADS, 128)
    w_uk, w_uv = kvb[:, :, :64].reshape(KVL, D), kvb[:, :, 64:].reshape(KVL, D)
    mla_w = con(np.concatenate([w_uk.reshape(2, P, D).transpose(1, 0, 2).reshape(P, -1),
                                w_uv.reshape(2, P, D).transpose(1, 0, 2).reshape(P, -1),
                                w_uk.T.reshape(DC, P, KVL).transpose(1, 0, 2).reshape(P, -1)], 1))
    ckv_pool = f["cache_ckv"][0]
    cache_t = con(np.concatenate([ckv_pool.transpose(0, 2, 1).reshape(POOL, 2, P, P).transpose(0, 2, 1, 3),
                                  np.tile(f["cache_kpe"][0].transpose(0, 2, 1), (1, 4, 1))[:, :, None, :]], 2)
                  ).reshape(POOL, P, 3 * P)
    state = con(f["state_wkv"][0].reshape(P, 64 * 64))
    page_table = con(f["page_table"].reshape(1, PAGES))

    ins = {"x_t": x_t.reshape(P, -1), "shift_t": shift_t, "vecs": vecs, "consts": consts, "wmasks": wmasks,
           "rope": rope, "wstream": wstream, "sub_keys": sub_keys, "mla_w": mla_w, "page_table": page_table,
           "cache_t": cache_t, "cache_n": con(ckv_pool), "state": state}
    outs = {"y": (P, DC * T), "ckv": (P, 2, T), "kpe": (ROPE, T), "wkv_p": (P, DC, 64), "shift": (P, DC, NS + 1),
            "wkv_s": (P, 64 * 64)}
    nc = _bacc.Bacc("TRN2", target_bir_lowering=False, num_devices=1)
    args, arrays = [], {}
    for n, a in ins.items():
        arrays[f"in_{n}"] = a
        args.append(nc.dram_tensor(f"in_{n}", a.shape, mybir.dt.from_np(a.dtype), kind="ExternalInput").ap())
    for n, shape in outs.items():
        args.append(nc.dram_tensor(f"out_{n}", shape, F32, kind="ExternalOutput").ap())
    build(nc, *args)
    r = _run(nc, [arrays], core_ids=[0]).results[0]
    got = {n: r[f"out_{n}"] for n in outs}
    y = got["y"].reshape(P, DC, T).transpose(2, 1, 0).reshape(T, D)
    ckv = got["ckv"].transpose(2, 1, 0).reshape(T, KVL)
    kpe = got["kpe"].T
    shift = got["shift"].transpose(2, 1, 0).reshape(NS + 1, D)
    wkv_p = got["wkv_p"].reshape(2, 64, DC, 64).transpose(2, 0, 3, 1).reshape(HEADS, 64, 64)
    c = con
    return (c(y[:NP_])[None], c(y[NP_:])[:, None], c(ckv[:NP_])[None, None], c(kpe[:NP_])[None, None],
            c(wkv_p)[None, None], c(shift[:1])[None], c(ckv[NP_:])[None, :, None], c(kpe[NP_:])[None, :, None],
            c(got["wkv_s"].reshape(1, NS, HEADS, 64, 64)), c(shift[1:])[None])
```

```python
from contextlib import ExitStack

import numpy as np

import concourse.bass as bass
from concourse import mybir

F32 = mybir.dt.float32
F32R = mybir.dt.float32r
BF16 = mybir.dt.bfloat16
I32 = mybir.dt.int32
U32 = mybir.dt.uint32
ALU = mybir.AluOpType
ACT = mybir.ActivationFunctionType
AX = mybir.AxisListType

P = 128
D = 1024
DC = D // P
NP_ = 256
NS = 8
T = NP_ + NS
HEADS = 16
CH = 64
NCH = NP_ // CH
QL, KVL, ROPE = 384, 256, 32
QC = QL // P
SCALE = (64 + 32) ** -0.5
EPS = 1e-6
GN_EPS = 64e-5
NPAGE = 16
PAGES = NS * NPAGE
POOL = (5 * PAGES + 3) // 4
NSLOT = 16
POOL_SLOTS = range(1, NSLOT - 1, 2)
PH = 8
TOPK = 16
TT = [(0, 128), (128, 128), (256, 8)]
NEG = -1e30
VERY_NEG = -3e38

RING = 8
TILES = {}
_n = 0
for _name, _count in [("r", 8), ("k", 8), ("v", 8), ("w1", 1), ("a1", 1), ("g1", 1), ("w2", 1), ("a2", 1), ("g2", 1),
                      ("rw_out", 8), ("wq0", 16), ("peer0", 256),
                      ("mla_in", 6), ("qb", 12), ("mla_out", 8), ("wq1", 16), ("peer1", 256)]:
    TILES[_name] = _n
    _n += _count
NTILES = _n
assert NTILES % RING == 0
GR = 2
HALF = P // 2
NG = HALF // GR
OHT = 8
OHS = 3

VECS = ["norm_mix0", "norm_mix1", "norm_ffn0", "norm_ffn1", "mu0", "mu1", "mu2", "mu3", "mu4", "mu5",
        "w0", "a0", "k_k", "k_a", "r_k", "ln_w", "ln_b"]
VCOL = {n: i * DC for i, n in enumerate(VECS)}
for _n2, _w in [("q_norm", 3), ("kv_norm", 2), ("qn_nope", 1), ("qn_rope", 1), ("kn_nope", 1), ("kn_rope", 1)]:
    VCOL[_n2] = max(VCOL.values()) + (DC if len(VCOL) == len(VECS) else _prev)
    _prev = _w
NV = VCOL["kn_rope"] + 1

CONSTS = ["ident", "ones", "bd64", "bd32", "rot", "iota", "stack", "half0", "half1", "quar0", "quar1", "quar2", "quar3"]
CCOL = {n: i * P for i, n in enumerate(CONSTS)}
CCOL["amask"] = len(CONSTS) * P
NCONST = (len(CONSTS) + 3) * P
WMASKS = ["strict", "incl"] + [f"level{i}" for i in range(6)]


def const_arrays():
    i = np.arange(P)
    eye = np.eye(P, dtype=np.float32)
    rot = np.zeros((P, P), np.float32)
    for m in range(P):
        if m % 32 < 16:
            rot[m + 16, m] = -1.0
        else:
            rot[m - 16, m] = 1.0
    causal = np.where(i[None, :] <= i[:, None], 0.0, NEG).astype(np.float32)
    mats = {"ident": eye, "ones": np.ones((P, P)), "bd64": i[:, None] // 64 == i[None, :] // 64,
            "bd32": i[:, None] // 32 == i[None, :] // 32, "rot": rot, "stack": i[:, None] % 64 == i[None, :], "iota": np.broadcast_to(i, (P, P))}
    for h in range(2):
        mats[f"half{h}"] = np.broadcast_to((i // 64 == h)[:, None], (P, P))
    for h in range(4):
        mats[f"quar{h}"] = np.broadcast_to((i // 32 == h)[:, None], (P, P))
    cols = [mats[n] for n in CONSTS] + [causal, np.zeros((P, P)), causal]
    s, t = i[:, None], i[None, :]
    same = s // CH == t // CH
    wm = [same & (s < t), same & (s <= t)]
    for lev in range(6):
        b = 1 << lev
        wm.append(-1.0 * ((s // (2 * b) == t // (2 * b)) & (s // b % 2 == 0) & (t // b % 2 == 1)))
    pos = np.concatenate([np.arange(NP_), np.full(NS, NPAGE * P)]).astype(np.float32)
    inv = np.float32(10000.0) ** (-np.arange(0, ROPE, 2, dtype=np.float32) / np.float32(ROPE))
    ang = (pos[None, :] * inv[i % 16][:, None].astype(np.float32)).astype(np.float32)
    rope = np.stack([np.cos(ang), np.sin(ang)], 1)
    f = lambda x: np.ascontiguousarray(np.concatenate([np.asarray(y, np.float32) for y in x], 1))
    return f(cols), f(wm), np.ascontiguousarray(rope.astype(np.float32))


class Seen:

    def __init__(self, eng):
        self.eng, self.n = eng, {}

    def next(self, sem, k=1):
        v = self.n.get(id(sem), 0) + k
        self.n[id(sem)] = v
        self.eng.wait_ge(sem, v)

    def passed(self, sem, k):
        self.n[id(sem)] = self.n.get(id(sem), 0) + k

    def count(self, sem):
        return self.n.get(id(sem), 0)


def build(nc, x_t, shift_t, vecs, consts, wmasks, rope, wstream, sub_keys, mla_w, page_table, cache_t, cache_n,
          state, y_out, ckv_out, kpe_out, wkv_p_out, shift_out, wkv_s_out):
    ctx = ExitStack()
    with ctx:
        def sb(name, cols, dt=F32):
            return ctx.enter_context(nc.sbuf_tensor(name, [P, cols], dt))

        def sem(name):
            return ctx.enter_context(nc.semaphore(name))

        ARENA = 35240
        arena = sb("arena", ARENA)
        arena_at = nc.sbuf_base - 4 * ARENA
        assert arena_at % 32 == 0
        ring = sb("ring", RING * D)
        xbuf = sb("xbuf", DC * T)
        xnbuf = sb("xnbuf", DC * T)
        hbuf = sb("hbuf", 2 * GR * T)
        cst = sb("cst", NCONST)
        vec = sb("vec", NV)
        skb = sb("skb", 4 * P)
        idxb = sb("idxb", 3 * T)
        rsb = sb("rsb", 3 * T)
        ps = ctx.enter_context(nc.psum_tensor("ps", [P, 8, 512], F32))
        scr_in = nc.dram_tensor("scr_in", [6, NS, D], F32).ap()
        scr_y = nc.dram_tensor("scr_y", [NS, D], F32).ap()

        xT = xbuf[:, :].rearrange("p (c t) -> p c t", c=DC)
        xn = xnbuf[:, :].rearrange("p (c t) -> p c t", c=DC)

        def C(name, n=P):
            return cst[:, CCOL[name]:CCOL[name] + n]

        def V(name, i=0, n=1):
            return vec[:, VCOL[name] + i:VCOL[name] + i + n]

        def vb(name, n=T):
            return V(name, 0, DC).unsqueeze(2).broadcast_to([P, DC, n])

        def slot(n):
            s = n % RING
            return ring[:, s * D:(s + 1) * D].rearrange("p (c m) -> p c m", c=DC)

        top = [0]

        def A(cols, *dims):
            a = arena[:, top[0]:top[0] + cols]
            top[0] += cols
            assert top[0] <= ARENA, top[0]
            if len(dims) == 2:
                return a.rearrange("p (a b) -> p a b", b=dims[1])
            if len(dims) == 3:
                return a.rearrange("p (a b c) -> p a b c", b=dims[1], c=dims[2])
            return a

        N3 = DC * T
        r_t, k_t, v_t, ld_t, a_t, g_t = (A(N3, DC, T) for _ in range(6))
        kk_t = A(N3, DC, T)
        bon_t = A(N3, DC, T)
        mix = [A(N3, DC, T) for _ in range(2)]
        xx = A(N3, DC, T)
        tmp_t = A(N3, DC, T)
        Rb = A(DC * NP_, DC, NP_)
        wm = A(8 * P, 8, P)
        smp = A(6 * DC * NS, 6, DC, NS)
        lam = A(DC * NCH, DC, NCH)
        lw, la, lg = (A(T) for _ in range(3))
        smp_row = A(6 * 64, 6, 64)
        shift_sb = lw[:, 0:DC * NS].rearrange("p (c b) -> p c b", c=DC)
        rw_top = top[0]

        def over(view, n, *dims):
            a = view.rearrange("p c t -> p (c t)")[:, 0:n]
            if len(dims) == 2:
                return a.rearrange("p (a b) -> p a b", b=dims[1])
            if len(dims) == 3:
                return a.rearrange("p (a b c) -> p a b c", b=dims[1], c=dims[2])
            return a

        cum = [over(mix[0], DC * NP_, DC, NP_), over(mix[1], DC * NP_, DC, NP_)]
        Kb = over(xx, DC * NP_, DC, NP_)
        Bb = over(tmp_t, DC * NP_, DC, NP_)
        kb = cum[0]
        y_t = r_t
        ETi = over(xx, DC * NCH * 64, DC, NCH, 64)
        Hk = over(mix[0], DC * NCH * 64, DC, NCH, 64)
        pt = [kk_t.rearrange("p c t -> p (c t)")[:, i * 512:(i + 1) * 512] for i in range(4)] + \
             [a_t.rearrange("p c t -> p (c t)")[:, i * 512:(i + 1) * 512] for i in range(4)] + \
             [ld_t.rearrange("p c t -> p (c t)")[:, i * 512:(i + 1) * 512] for i in range(4)]
        LT, MTm, ArkT, ArbT, Xs, XTs, Zs, RHS, BKrow, nWU, NTl0, NTl1 = pt
        NTl = [NTl0, NTl1]
        q4 = lambda a: a.rearrange("p (q n) -> p q n", q=4)
        mis = mix[1].rearrange("p c t -> p (c t)")
        Vrow = mis[:, 0:256].rearrange("p (j h v) -> p j h v", j=2, h=2)
        Pst = mis[:, 256:256 + 512].rearrange("p (c v) -> p c v", c=DC)
        st_q = [k_t.rearrange("p c t -> p (c t)")[:, i * D:(i + 1) * D].rearrange("p (v k) -> p v k", v=16) for i in range(2)]
        vflat = hbuf
        st_tmp = vflat[:, 0:D].rearrange("p (v k) -> p v k", v=16)
        skk = rsb[:, 0:16]
        y_smp = rsb[:, 64:128]
        top[0] = rw_top
        rows_sb = [A(2 * D)[0:NS, :], A(2 * D)[0:NS, :], Rb.rearrange("p c t -> p (c t)")[0:NS, :]]

        top[0] = 0
        G = arena[:, 0:HALF * T].rearrange("p (n t) -> p n t", n=HALF)
        split_at = HALF * T
        at = [arena_at + 4 * split_at]

        def halves(name, cols):
            a = nc.alloc_sbuf_tensor_at(name, [P, cols], F32R, offset=at[0])
            at[0] += 4 * cols
            assert at[0] <= arena_at + 4 * ARENA
            return a

        w_hi, w_lo = halves("w_hi", 4 * D), halves("w_lo", 4 * D)
        x_hi, x_lo = halves("x_hi", DC * T), halves("x_lo", DC * T)
        h_hi, h_lo = halves("h_hi", 2 * GR * T), halves("h_lo", 2 * GR * T)
        w_half = [[a[:, i * D:(i + 1) * D] for i in range(4)] for a in (w_hi, w_lo)]
        x_half = [a[:, :].rearrange("p (c t) -> p c t", c=DC) for a in (x_hi, x_lo)]
        h_half = [a[:, :].rearrange("p (g t) -> p g t", t=T) for a in (h_hi, h_lo)]
        PASSES = ((0, 0), (0, 1), (1, 0))
        set_words = OHT * (P + 4 * HALF) // 2
        oh = [arena[:, split_at + s * set_words:split_at + (s + 1) * set_words].bitcast(BF16) for s in range(OHS)]
        oh1 = [a[:, 0:OHT * P].rearrange("p (n u) -> p n u", u=OHT) for a in oh]
        oh2 = [a[:, OHT * P:OHT * (P + HALF)].rearrange("p (n u) -> p n u", u=OHT) for a in oh]
        oh2g = [a[:, OHT * (P + HALF):].rearrange("p (k n u) -> p k n u", k=3, u=OHT) for a in oh]
        top[0] = (at[0] - arena_at) // 4
        keys8 = A(OHT * P // 2).bitcast(BF16).rearrange("p (n u) -> p n u", u=OHT)
        idxh = A(5 * T // 2).bitcast(BF16).rearrange("p (k t) -> p k t", t=T)
        rest = A(T)
        top[0] = 0
        S = A(3 * 16 * P, 3, 16, P)
        S2 = A(6 * P, 6, P)
        v16 = A(3 * 16 * TOPK, 3, 16, TOPK)
        i16u = A(3 * 16 * TOPK).bitcast(U32).rearrange("p (i g k) -> p i g k", i=3, g=16)
        i16f = A(3 * 16 * TOPK, 3, 16, TOPK)
        cand = A(3 * 256, 3, 256)
        cand2 = A(3 * 256, 3, 256)
        eqs = [A(PH * 256, PH, 256) for _ in range(3)]
        ts16 = A(3 * PH * TOPK, 3, PH, TOPK)
        posu = A(3 * PH * TOPK).bitcast(U32).rearrange("p (i g k) -> p i g k", i=3, g=PH)
        abu = A(3 * 2 * P).bitcast(U32).rearrange("p (i two n) -> p i two n", i=3, two=2)
        abf = A(3 * 2 * P, 3, 2, P)
        sel = A(3 * 3 * P, 3, 3, P)
        smax = A(3 * PH, 3, PH, 1)
        qb = [A(T), A(T)]
        key_of = lambda i, k, nt: i16f[0:nt, i].rearrange("p (h two) k -> p h two k", two=2)[:, :, k, :
                                                          ].unsqueeze(2).broadcast_to([nt, PH, TOPK, TOPK])
        eq_rows = lambda e, nt: e[0:nt].rearrange("p h (a b) -> p h a b", a=TOPK)
        EQ_JOBS = ((0, 0), (0, 1), (1, 0), (1, 1))
        idx = idxb[:, :].rearrange("p (k t) -> p k t", k=3)
        hg = hbuf[:, :].rearrange("p (g t) -> p g t", t=T)

        top[0] = 0
        w_uk = A(2 * D, 2, D)
        w_uv = A(2 * D, 2, D)
        w_ukT = A(DC * KVL, DC, KVL)
        cs = A(2 * T, 2, T)
        cq = A(3 * T, 3, T)
        ckv = A(2 * T, 2, T)
        kp = A(T)
        qn_at = top[0]
        qn = A(N3, DC, T)
        kn_at = top[0]
        kn = A(N3, DC, T)
        qr = A(4 * T, 4, T)
        sqb = A(N3, DC, T)
        rs8 = A(N3, DC, T)
        vr_at = top[0]
        vr = A(2 * D, 2, D)
        o_t = A(N3, DC, T)
        qm = [A(512, 2, 256) for _ in range(2)]
        Sm = [A(384) for _ in range(2)]
        PTs = [A(384) for _ in range(2)]
        mxl = [A(8) for _ in range(2)]
        o_row = A(2 * D, 2, D)
        qgm = A(DC * 2 * NS, DC, 2, NS)
        qp = A(2 * NS * HEADS, 2, NS, HEADS)
        qrz = A(NS * HEADS, NS, HEADS)
        prodn = A(DC * NS, DC, NS)
        prodr = A(4 * NS, 4, NS)
        NPG = PAGES * HEADS
        SN = A(2 * NPG, PAGES, 2 * HEADS)
        SS = A(NPG, PAGES, HEADS)
        sqp = [o_row[:, j, :] for j in range(2)]
        small = A(10 * P, 10, P)
        cpT = [x.rearrange("p (a b) -> p a b", a=3) for x in Sm + PTs]
        accT = A(2 * P, 2, NS, HEADS)
        cnew = A(2 * P, 2, NS, HEADS)
        PR = rs8.rearrange("p c t -> p (c t)")[:, 0:NPG].rearrange("p (g h) -> p g h", h=HEADS)
        cpN = [a[:, i * KVL:(i + 1) * KVL] for a in (sqb.rearrange("p c t -> p (c t)"),
                                                     w_ukT.rearrange("p c n -> p (c n)")) for i in range(8)]
        at[0] = arena_at + 4 * vr_at
        uk_hi = halves("uk_hi", 2 * D)
        at[0] = arena_at + 4 * kn_at
        uk_lo = halves("uk_lo", 2 * D)
        at[0] = arena_at + 4 * qn_at
        pg_hi, pg_lo = halves("pg_hi", 4 * KVL), halves("pg_lo", 4 * KVL)
        uk_half = [a[:, :].rearrange("p (c n) -> p c n", c=2) for a in (uk_hi, uk_lo)]
        pg_half = [a[:, :].rearrange("p (g c n) -> p g c n", g=4, c=2) for a in (pg_hi, pg_lo)]
        ptab = ctx.enter_context(nc.sbuf_tensor("ptab", [1, PAGES], I32))

        consts_in = sem("consts_in")
        slot_in = [sem(f"slot_in{i}") for i in range(RING)]
        tile_used = sem("tile_used")
        bank_free = [sem(f"bank_free{i}") for i in range(8)]
        for_act = sem("for_act")
        for_dve = sem("for_dve")
        dve_step = sem("dve_step")
        act_step = sem("act_step")
        sq_ready = sem("sq_ready")
        rsq_in = sem("rsq_in")
        rsq_out = sem("rsq_out")
        xn_ready = sem("xn_ready")
        mix_ready = sem("mix_ready")
        lora_ready = sem("lora_ready")
        stat_ready = sem("stat_ready")
        proj_copied = sem("proj_copied")
        smp_ready = sem("smp_ready")
        smp_rows = sem("smp_rows")
        smp_out = sem("smp_out")
        smp_back = sem("smp_back")
        st_in = [sem(f"st_in{i}") for i in range(2)]
        st_done = sem("st_done")
        st_out = sem("st_out")
        ysm_out = sem("ysm_out")
        ysm_back = sem("ysm_back")
        ysm_T = sem("ysm_T")
        ld_scaled = sem("ld_scaled")
        cum_ready = sem("cum_ready")
        e_ready = sem("e_ready")
        ops_ready = sem("ops_ready")
        rows_act = sem("rows_act")
        rows_dve = sem("rows_dve")
        nt_ready = sem("nt_ready")
        lt_ready = sem("lt_ready")
        z_ready = sem("z_ready")
        x_ready = sem("x_ready")
        xt_ready = sem("xt_ready")
        rhs_ready = sem("rhs_ready")
        nwu_ready = sem("nwu_ready")
        ab_ready = sem("ab_ready")
        pair_done = sem("pair_done")
        state_ready = sem("state_ready")
        y_ready = sem("y_ready")
        yg_ready = sem("yg_ready")
        x_added = sem("x_added")
        q_copied = sem("q_copied")
        s_copied = sem("s_copied")
        sel_ready = sem("sel_ready")
        eq_made = sem("eq_made")
        eq_keys = sem("eq_keys")
        oh_ready = sem("oh_ready")
        oh_used = sem("oh_used")
        oh1_made = sem("oh1_made")
        oh2_made = sem("oh2_made")
        idx_ready = sem("idx_ready")
        xhi_ready = sem("xhi_ready")
        hi_ready = sem("hi_ready")
        gated = sem("gated")
        hhi_ready = sem("hhi_ready")
        gelu_done = sem("gelu_done")
        h_ready = sem("h_ready")
        shift_sent = sem("shift_sent")
        wkv_sent = sem("wkv_sent")
        lat_sent = sem("lat_sent")
        y_sent = sem("y_sent")
        pr_exp = sem("pr_exp")
        gate_in = sem("gate_in")
        gate_exp = sem("gate_exp")
        smp_decay = sem("smp_decay")
        mla_in = sem("mla_in")
        kp_ready = sem("kp_ready")
        lat_ready = sem("lat_ready")
        heads_ready = sem("heads_ready")
        qm_ready = sem("qm_ready")
        neg_ready = sem("neg_ready")
        p_ready = sem("p_ready")
        pt_ready = sem("pt_ready")
        o_ready = sem("o_ready")
        oT_copied = sem("oT_copied")
        qs_ready = sem("qs_ready")
        qp_ready = sem("qp_ready")
        page_in = [sem(f"page_in{i}") for i in range(4)]
        page_used = sem("page_used")
        sqp_ready = sem("sqp_ready")
        sqp_used = sem("sqp_used")
        m1_ready = sem("m1_ready")
        dg_ready = sem("dg_ready")
        pr_in = sem("pr_in")
        natp_in = [sem(f"natp_in{i}") for i in range(NSLOT)]
        ukhi_ready = sem("ukhi_ready")
        uk_ready = sem("uk_ready")
        pghi_ready = sem("pghi_ready")
        pg_ready = sem("pg_ready")
        natp_used = sem("natp_used")
        acc_ready = sem("acc_ready")
        oall_ready = sem("oall_ready")

        block = ctx.enter_context(nc.Block())
        marks = {}
        for_dve_before = {}

        def page(eng, stream, at, dst, signal):
            phys = eng.value_load(ptab[0:1, bass.ds(at, 1)], min_val=0, max_val=POOL - 1)
            eng.dma_start(dst, stream[bass.ds(phys, 1), :, :].rearrange("o p n -> (o p) n")).then_inc(signal, 16)

        @block.sync
        def _(sp):
            w = Seen(sp)
            sp.dma_start(xbuf[:, :], x_t).then_inc(consts_in, 16)
            sp.dma_start(vec[:, :], vecs).then_inc(consts_in, 16)
            sp.dma_start(cst[:, :], consts).then_inc(consts_in, 16)
            sp.dma_start(shift_sb, shift_t).then_inc(consts_in, 16)
            sp.dma_start(skb[:, :], sub_keys).then_inc(consts_in, 16)
            sp.dma_start(wm.rearrange("p a b -> p (a b)"), wmasks).then_inc(consts_in, 16)
            sp.dma_start(ptab[:, :], page_table).then_inc(consts_in, 16)
            for n in range(RING):
                sp.dma_start(ring[:, n * D:(n + 1) * D], wstream[n, :, :]).then_inc(slot_in[n], 16)
            with sp.Fori(1, NTILES // RING) as rnd:
                for n in range(RING):
                    sp.wait_ge(tile_used, rnd * RING + (n + 1 - RING))
                    sp.dma_start(ring[:, n * D:(n + 1) * D],
                                 wstream[bass.ds(rnd * RING + n, 1), :, :].rearrange("o p n -> (o p) n")
                                 ).then_inc(slot_in[n], 16)

        @block.gpsimd
        def _(pool):
            w = Seen(pool)

            def gate_rows(layer):
                for j, (i, k) in enumerate(EQ_JOBS):
                    w.next(eq_made)
                    nc.gpsimd.tensor_tensor(eq_rows(eqs[j % 2], P), eq_rows(eqs[j % 2], P), key_of(i, k, P), ALU.mult
                                            ).then_inc(eq_keys, 1)
                for hf in range(2):
                    sets0 = (2 * layer + hf) * (T // OHT)
                    with pool.Fori(0, T // OHT // OHS) as it:
                        for st in range(OHS):
                            pool.wait_ge(oh2_made, it * OHS + (sets0 + st + 1))
                            nc.gpsimd.tensor_tensor(
                                oh2g[st][:, 2], oh2[st], idxh[:, 4, bass.ds(it * (OHT * OHS) + st * OHT, OHT)
                                                              ].unsqueeze(1).broadcast_to([P, HALF, OHT]), ALU.mult
                                ).then_inc(oh_ready, 1)

            w.next(xn_ready)
            pool.dma_start(shift_out, xn[:, :, NP_ - 1:T]).then_inc(shift_sent, 16)
            for g in range(3):
                pool.wait_ge(smp_rows, 4 * (g + 1))
                pool.dma_start(scr_in[2 * g:2 * g + 2].rearrange("j b n -> b j n"),
                               rows_sb[g].rearrange("b (j n) -> b j n", j=2)).then_inc(smp_out, 16)
            pool.wait_ge(smp_out, 48)
            for j in range(6):
                pool.dma_start(smp_row[:, j, :], scr_in[j].rearrange("b (h v) -> (b h) v", h=HEADS)
                               ).then_inc(smp_back, 16)
            pool.wait_ge(ops_ready, 1)
            for qd in range(4):
                if qd >= 2:
                    pool.wait_ge(st_out, 16 * (qd - 1))
                pool.dma_start(st_q[qd % 2].rearrange("p v k -> p (v k)"), state[:, qd * D:(qd + 1) * D]).then_inc(st_in[qd % 2], 16)
                if qd >= 1:
                    pool.wait_ge(st_done, qd)
                    pool.dma_start(wkv_s_out[:, (qd - 1) * D:qd * D],
                                   st_q[(qd - 1) % 2].rearrange("p v k -> p (v k)")).then_inc(st_out, 16)
            pool.wait_ge(st_done, 4)
            pool.dma_start(wkv_s_out[:, 3 * D:4 * D], st_q[1].rearrange("p v k -> p (v k)")).then_inc(st_out, 16)
            pool.dma_start(scr_y.rearrange("b (h v) -> (b h) v", h=HEADS), y_smp).then_inc(ysm_out, 16)
            pool.wait_ge(ysm_out, 16)
            pool.dma_start(rows_sb[0][:, 0:D], scr_y).then_inc(ysm_back, 16)
            pool.wait_ge(state_ready, NCH)
            pool.dma_start(wkv_p_out, Pst).then_inc(wkv_sent, 16)
            pool.wait_ge(st_out, 64)
            gate_rows(0)
            pool.wait_ge(x_added, 2)
            pool.dma_start(arena[:, 0:2 * 2 * D + DC * KVL], mla_w).then_inc(mla_in, 16)
            pool.dma_start(cs.rearrange("p a b -> p (a b)"), rope.rearrange("p a b -> p (a b)")).then_inc(mla_in, 16)
            pool.wait_ge(kp_ready, 1)
            pool.dma_start(ckv_out, ckv).then_inc(lat_sent, 16)
            pool.dma_start(kpe_out, kp[0:ROPE, :]).then_inc(lat_sent, 16)
            pool.wait_ge(qp_ready, 1)

            for n in range(4):
                page(pool, cache_t, n, cpT[n].rearrange("p a b -> p (a b)"), page_in[n])
            with pool.Fori(1, PAGES // 4) as it:
                for n in range(4):
                    pool.wait_ge(page_used, it * 4 + (n - 3))
                    page(pool, cache_t, it * 4 + n, cpT[n].rearrange("p a b -> p (a b)"), page_in[n])
            for n in POOL_SLOTS:
                page(pool, cache_n, n, cpN[n], natp_in[n])
            with pool.Fori(1, PAGES // NSLOT) as it:
                for n in POOL_SLOTS:
                    pool.wait_ge(natp_used, it * NSLOT + (n + 1 - NSLOT))
                    page(pool, cache_n, it * NSLOT + n, cpN[n], natp_in[n])
            gate_rows(1)
            pool.wait_ge(x_added, 4)
            pool.dma_start(y_out, xbuf[:, :]).then_inc(y_sent, 16)
            pool.wait_ge(shift_sent, 16)
            pool.wait_ge(wkv_sent, 16)
            pool.wait_ge(lat_sent, 32)
            pool.wait_ge(y_sent, 16)


        @block.tensor
        def _(pe):
            w = Seen(pe)
            taken = [0] * 8

            def take(b, n=1):
                if taken[b]:
                    pe.wait_ge(bank_free[b], taken[b])
                taken[b] += n

            def tile(n):
                pe.wait_ge(slot_in[n % RING], 16 * (n // RING + 1))
                return slot(n)

            def mm(out, lhsT, rhs, start=True, stop=True, **kw):
                return nc.tensor.matmul(out, lhsT, rhs, start=start, stop=stop, **kw)

            def group_sums(src, n, lhsT):
                for i in range(n):
                    take(i)
                    mm(ps[:, i, 0:T], lhsT, src[:, i, :]).then_inc(for_dve, 1)

            def row_norm():
                w.next(sq_ready)
                take(0)
                for c in range(DC):
                    last = mm(ps[:, 0, 0:T], C("ones"), xn[:, c, :], c == 0, c == DC - 1)
                last.then_inc(for_dve, 1)

            def project(first, n, src, banks=(0, 1, 2, 3), kc=DC, rows=P):
                for o in range(n):
                    b = banks[o % len(banks)]
                    take(b)
                    wt = tile(first + o)
                    for c in range(kc):
                        last = mm(ps[0:rows, b, 0:T], wt[:, c, 0:rows], src[:, c, :], c == 0, c == kc - 1)
                    last.then_inc(tile_used, 1)

            def turn(out, src, rows=P):
                return nc.tensor.transpose(out, src, C("ident")[0:rows, 0:rows])

            def peer(layer):
                first = TILES[f"wq{layer}"]
                w.next(xn_ready)
                for g in range(16 + 1):
                    if g < 16:
                        take(g % 2)
                        wt = tile(first + g)
                        for c in range(DC):
                            last = mm(ps[:, g % 2, 0:T], wt[:, c, :], xn[:, c, :], c == 0, c == DC - 1)
                        last.then_inc(tile_used, 1)
                    if g >= 1:
                        w.next(q_copied)
                        take(2 + g % 2)
                        for i, (t0, nt) in enumerate(TT):
                            kc = (2 * layer + (g - 1) % 2) * P
                            last = mm(ps[0:nt, 2 + g % 2, i * P:(i + 1) * P], qb[(g - 1) % 2][:, t0:t0 + nt],
                                      skb[:, kc:kc + P])
                        last.then_inc(for_act, 1)
                for i, (t0, nt) in enumerate(TT):
                    w.next(sel_ready)
                    take(i)
                    for k in range(3):
                        last = turn(ps[:, i, k * P:k * P + nt], sel[0:nt, i, k, :], nt)
                    last.then_inc(for_dve, 1)
                for hf in range(2):
                    experts(layer, hf)

            def experts(layer, hf):
                k = 2 * layer + hf
                pe.sem_inc(oh_used, OHS)
                sets0, free0 = k * (T // OHT), list(taken)
                with pe.Fori(0, T // OHT // OHS) as it:
                    for st in range(OHS):
                        pe.wait_ge(bank_free[st], it + free0[st])
                        pe.wait_ge(oh_ready, it * OHS + (sets0 + st + 1))
                        pe.wait_ge(oh1_made, it * OHS + (sets0 + st + 1))
                        for u in range(OHT):
                            for n in range(3):
                                last = mm(ps[:, st, u * HALF:(u + 1) * HALF], oh1[st][:, :, u], oh2g[st][:, n, :, u],
                                          n == 0, n == 2)
                        last.then_inc(oh_used, 1)
                for b in range(OHS):
                    taken[b] += T // OHT // OHS
                t0 = TILES[f"peer{layer}"] + 2 * HALF * hf
                base = list(taken)
                marks[k] = base

                def hidden(g, at, it=0):
                    for u in range(GR):
                        b = 2 * (g % 2) + u
                        pe.wait_ge(bank_free[b], it + (base[b] + g // 2))
                        pe.wait_ge(tile_used, it * 8 + (t0 + at + u + 1))
                        for c in range(DC):
                            for n, (i, j) in enumerate(PASSES):
                                last = mm(ps[:, b, 0:T], w_half[i][(at + u) % 4][:, c * P:(c + 1) * P],
                                          x_half[j][:, c, :], c + n == 0, c == DC - 1 and n == 2)
                        last.then_inc(for_act, 1)

                def outputs(g, at, it=0):
                    pe.wait_ge(h_ready, it * 2 + (k * NG + g + 1))
                    pe.wait_ge(tile_used, it * 8 + (t0 + at + GR))
                    for c in range(DC):
                        b = 4 + c % 4
                        pe.wait_ge(bank_free[b], it * 4 + (base[b] + 2 * g + c // 4))
                        for u in range(GR):
                            for n, (i, j) in enumerate(PASSES):
                                last = mm(ps[:, b, 0:T], w_half[i][(at + u) % 4][:, c * P:(c + 1) * P],
                                          h_half[j][:, g % 2 * GR + u, :], u + n == 0, u == GR - 1 and n == 2)
                        last.then_inc(for_dve, 1)

                hidden(0, 0)
                hidden(1, 2)
                with pe.Fori(0, NG // 2 - 1) as it:
                    for g in range(2):
                        outputs(g, 4 * g + 4, it)
                        hidden(g + 2, 4 * g + 6, it)
                outputs(NG - 2, 4 * NG - 4)
                outputs(NG - 1, 4 * NG - 2)
                for b in range(4):
                    taken[b] += NG // 2
                for b in range(4, 8):
                    taken[b] += 2 * NG

            pe.wait_ge(consts_in, 16 * 7)
            row_norm()
            w.next(xn_ready)
            for m, name in enumerate(["r", "k", "v"]):
                w.next(mix_ready)
                project(TILES[name], 8, mix[m % 2])
            for m, (name, rows) in enumerate([("w1", 64), ("a1", 64), ("g1", 128)]):
                w.next(mix_ready)
                project(TILES[name], 1, mix[(3 + m) % 2], banks=(m,), rows=rows)
            for name, src, rows in [("w2", lw, 64), ("a2", la, 64), ("g2", lg, 128)]:
                w.next(lora_ready)
                wt = tile(TILES[name])
                for o in range(DC):
                    take(o % 4)
                    last = mm(ps[:, o % 4, 0:T], wt[0:rows, o, :], src[0:rows, :])
                    last.then_inc(tile_used if o == DC - 1 else for_act, 1)
            w.next(stat_ready)
            group_sums(tmp_t, DC, C("bd64"))
            w.next(stat_ready)
            group_sums(tmp_t, DC, C("bd64"))
            w.next(smp_ready)
            for j in range(6):
                for half in range(2):
                    b = (2 * j + half) % 4
                    take(b)
                    for c in range(4):
                        last = turn(ps[0:NS, b, c * P:(c + 1) * P], smp[:, j, half * 4 + c, :])
                    last.then_inc(for_act, 1)
            w.next(ops_ready)
            for c in range(DC):
                take(0)
                for i, src in enumerate([v_t, Kb]):
                    for j in range(2):
                        last = turn(ps[:, 0, (2 * i + j) * P:(2 * i + j + 1) * P], src[:, c, j * P:(j + 1) * P])
                last.then_inc(for_act, 1)
                take(1)
                for i, src in enumerate([Bb, kb]):
                    for j in range(2):
                        last = turn(ps[:, 1, (2 * i + j) * P:(2 * i + j + 1) * P], src[:, c, j * P:(j + 1) * P])
                last.then_inc(for_dve, 1)
                for bank0, moving in ((2, Kb), (4, Rb)):
                    for h in range(2):
                        take(bank0 + h)
                        pr = slice(64 * h, 64 * h + 64)
                        for i, stat in enumerate([Bb, kb]):
                            for j in range(2):
                                cols = slice(j * P, (j + 1) * P)
                                last = mm(ps[:, bank0 + h, (2 * i + j) * P:(2 * i + j + 1) * P],
                                          stat[pr, c, cols], moving[pr, c, cols])
                        last.then_inc(for_dve, 1)
                w.next(rows_act)
                w.next(ab_ready)
                take(6)
                for q in range(4):
                    last = mm(ps[:, 6, q * 64:(q + 1) * 64], q4(MTm)[:, q, :], Vrow[:, q % 2, q // 2, :])
                last.then_inc(for_act, 1)
                take(2)
                take(3)
                id4 = C("ident").unsqueeze(1).broadcast_to([P, 4, P])
                w.next(nt_ready)
                acc = dict(start=False, stop=True, skip_group_check=True)
                mm(ps[:, 2, :], C("ident"), id4, stop=True, skip_group_check=True)
                for q in range(4):
                    last = nc.tensor.matmul(ps[:, 2, q * P:(q + 1) * P], q4(NTl[0])[:, q, :], C("ident"), **acc)
                last.then_inc(for_act, 1)
                mm(ps[:, 3, :], C("ident"), id4, stop=True, skip_group_check=True)
                nc.tensor.matmul(ps[:, 3, :], C("ident"), NTl[0], **acc).then_inc(for_dve, 1)
                for lev in range(1, 6):
                    w.next(nt_ready)
                    w.next(x_ready)
                    take(7)
                    for q in range(4):
                        last = mm(ps[:, 7, q * P:(q + 1) * P], q4(NTl[lev % 2])[:, q, :], q4(Xs)[:, q, :])
                    last.then_inc(for_act, 1)
                    w.next(z_ready)
                    w.next(xt_ready)
                    for q in range(4):
                        last = nc.tensor.matmul(ps[:, 2, q * P:(q + 1) * P], q4(XTs)[:, q, :], q4(Zs)[:, q, :], **acc)
                    last.then_inc(for_act, 1)
                    for q in range(4):
                        last = nc.tensor.matmul(ps[:, 3, q * P:(q + 1) * P], q4(Zs)[:, q, :], q4(XTs)[:, q, :], **acc)
                    last.then_inc(for_dve, 1)
                w.next(xt_ready)
                w.next(rhs_ready)
                take(0)
                for q in range(4):
                    last = mm(ps[:, 0, q * P:(q + 1) * P], q4(XTs)[:, q, :], q4(RHS)[:, q, :])
                last.then_inc(for_act, 1)
                w.next(rows_dve)
                w.next(nwu_ready)
                take(1)
                take(4)
                take(5)
                take(6)
                for h in range(2):
                    pr = slice(64 * h, 64 * h + 64)
                    for j in range(2):
                        q = 2 * h + j
                        mm(ps[pr, 1, j * P:(j + 1) * P], q4(nWU)[:, q, 0:64], q4(ArbT)[:, q, :])
                        mm(ps[pr, 4, j * P:(j + 1) * P], Vrow[:, j, h, :], q4(ArkT)[:, q, :], True, False)
                        mm(ps[pr, 4, j * P:(j + 1) * P], q4(nWU)[:, q, 64:128], q4(ArbT)[:, q, :], False, True)
                BK = BKrow.rearrange("p (i j h k) -> p i j h k", i=2, j=2, h=2)
                for h in range(2):
                    pr = slice(64 * h, 64 * h + 64)
                    for j in range(2):
                        q = 2 * h + j
                        for half in range(2):
                            b, rw = 5 + half, slice(64 * half, 64 * half + 64)
                            mm(ps[pr, b, j * 64:(j + 1) * 64], q4(nWU)[rw, q, 0:64], BK[rw, 0, j, h, :])
                            o = ps[pr, b, 256 + j * 64:256 + (j + 1) * 64]
                            mm(o, BK[rw, 1, j, h, :], Vrow[rw, j, h, :], True, False)
                            last = mm(o, BK[rw, 0, j, h, :], q4(nWU)[rw, q, 64:128], False, True)
                last.then_inc(for_dve, 1)
                w.next(pair_done)
            for cc in range(1, NCH):
                w.next(state_ready)
                cols = slice(cc * 64, cc * 64 + 64)
                for kind in range(2):
                    for h in range(2):
                        b = 2 * kind + h
                        take(b)
                        pr = slice(64 * h, 64 * h + 64)
                        for c in range(DC):
                            if kind == 0:
                                last = mm(ps[pr, b, c * 64:(c + 1) * 64], Pst[pr, c, :], Rb[pr, c, cols])
                            else:
                                last = mm(ps[pr, b, c * 64:(c + 1) * 64], ETi[pr, c, cc, :], Pst[pr, c, :])
                        last.then_inc(for_dve, 1)
            w.next(ysm_back, 16)
            take(4)
            for c in range(DC):
                last = turn(ps[:, 4, c * NS:(c + 1) * NS], rows_sb[0][:, c * P:(c + 1) * P], NS)
            last.then_inc(for_dve, 1)
            w.next(stat_ready)
            group_sums(y_t, DC, C("bd64"))
            w.next(stat_ready)
            group_sums(tmp_t, DC, C("bd64"))
            w.next(yg_ready)
            project(TILES["rw_out"], 8, y_t)
            row_norm()
            peer(0)

            row_norm()
            w.next(xn_ready)
            project(TILES["mla_in"], 6, xn)
            w.next(sq_ready)
            take(0)
            for c in range(3):
                last = mm(ps[:, 0, 0:T], C("ones"), sqb[:, c, :], c == 0, c == 2)
            last.then_inc(for_dve, 1)
            take(1)
            for c in range(2):
                last = mm(ps[:, 1, 0:T], C("ones"), sqb[:, 3 + c, :], c == 0, c == 1)
            last.then_inc(for_dve, 1)
            take(2)
            mm(ps[:, 2, 0:T], C("bd32"), sqb[:, 5, :]).then_inc(for_dve, 1)
            w.next(lat_ready)
            take(3)
            mm(ps[:, 3, 0:T], C("rot"), kp).then_inc(for_dve, 1)
            w.next(mla_in, 32)
            project(TILES["qb"], 12, cq, kc=QC)
            for o in range(DC):
                take(o % 4)
                for c in range(2):
                    last = mm(ps[:, o % 4, 0:T], w_uk[:, c, o * P:(o + 1) * P], ckv[:, c, :], c == 0, c == 1)
                last.then_inc(for_act, 1)
            for j in range(2):
                for half in range(2):
                    b = 2 * j + half
                    take(b)
                    for c in range(2):
                        last = mm(ps[:, b, :], ckv[:, c, j * P:(j + 1) * P], w_uv[:, c, half * 512:(half + 1) * 512],
                                  c == 0, c == 1)
                    last.then_inc(for_act, 1)
            for n, mat in ((DC, "bd64"), (DC, "bd64"), (4, "bd32")):
                w.next(stat_ready)
                group_sums(sqb, n, C(mat))
            w.next(heads_ready)
            for i in range(4):
                take(i)
                mm(ps[:, i, 0:T], C("rot"), qr[:, i, :]).then_inc(for_dve, 1)
            w.next(heads_ready)
            for i in range(HEADS + 1):
                if i < HEADS:
                    s, c = i % 2, i // 2
                    w.next(qm_ready)
                    take(s)
                    for j in range(2):
                        o = ps[:, s, j * P:j * P + (j + 1) * P]
                        mm(o, qm[s][:, 0, j * P:(j + 1) * P], kn[:, c, 0:(j + 1) * P], True, False)
                        last = mm(o, qm[s][:, 1, j * P:(j + 1) * P], kp[:, 0:(j + 1) * P], False, True)
                    last.then_inc(for_dve, 1)
                if i >= 1:
                    h = i - 1
                    s = h % 2
                    w.next(p_ready)
                    take(2 + s)
                    for k in range(3):
                        last = turn(ps[:, 2 + s, k * P:(k + 1) * P], Sm[s][:, k * P:(k + 1) * P])
                    last.then_inc(for_act, 1)
                    w.next(pt_ready)
                    take(4 + s)
                    hv = slice(h * 64, h * 64 + 64)
                    mm(ps[:, 4 + s, 0:64], PTs[s][:, 0:P], vr[:, 0, hv])
                    mm(ps[:, 4 + s, 64:128], PTs[s][:, P:2 * P], vr[:, 0, hv], True, False)
                    mm(ps[:, 4 + s, 64:128], PTs[s][:, 2 * P:3 * P], vr[:, 1, hv], False, True).then_inc(for_dve, 1)
            w.next(o_ready)
            for j in range(2):
                for half in range(2):
                    b = 2 * j + half
                    take(b)
                    for c in range(4):
                        cc = half * 4 + c
                        last = turn(ps[:, b, c * P:(c + 1) * P], o_row[:, j, cc * P:(cc + 1) * P])
                    last.then_inc(for_act, 1)
            w.next(qs_ready)
            take(0)
            for cc in range(2):
                for c in range(DC):
                    o = cc * P + c * 16
                    last = mm(ps[:, 0, o:o + 16], w_ukT[:, c, cc * P:(cc + 1) * P],
                              qgm[:, c, :, :].rearrange("p h b -> p (h b)"))
            last.then_inc(for_dve, 1)
            take(1)
            for h in range(HEADS):
                o = ps[:, 1, h * NS:(h + 1) * NS]
                mm(o, C(f"half{h % 2}"), prodn[:, h // 2, :], True, False)
                last = mm(o, C(f"quar{h % 4}"), prodr[:, h // 4, :], False, True)
            last.then_inc(for_dve, 1)
            w.next(qp_ready)
            base = list(taken)
            marks["pages"] = base
            w.next(uk_ready)
            for b in (1, 3):
                pe.wait_ge(bank_free[b], taken[b])
            with pe.Fori(0, PAGES // 4) as it:
                for n in range(4):
                    pg = cpT[n]
                    b = 2 * (n % 2)
                    pe.wait_ge(page_in[n], it * 16 + 16)
                    pe.wait_ge(pg_ready, it * 4 + (n + 1))
                    pe.wait_ge(bank_free[b], it * 2 + (base[b] + n // 2))
                    for half in range(2):
                        for c in range(2):
                            for m, (i, j) in enumerate(PASSES):
                                last = mm(ps[:, b + half, :], pg_half[i][:, n, c, :],
                                          uk_half[j][:, c, half * 512:(half + 1) * 512], c + m == 0, c == 1 and m == 2)
                    last.then_inc(for_act, 1)
                    sbk = 4 + n % 2
                    pe.wait_ge(bank_free[sbk], it * 2 + (base[sbk] + n // 2))
                    req = it // 4
                    for c in range(2):
                        mm(ps[:, sbk, 0:16], pg[:, c, :], qp[:, c, bass.ds(req, 1), :].rearrange("p o h -> p (o h)"),
                           c == 0, c == 1)
                    mm(ps[:, sbk, 16:32], pg[:, 2, :], qrz[:, bass.ds(req, 1), :].rearrange("p o h -> p (o h)")
                       ).then_inc(page_used, 1)
            for b in (0, 2, 4, 5):
                taken[b] += PAGES // 2
            w.next(m1_ready)
            take(6)
            turn(ps[:, 6, 0:P], small[:, 0, :]).then_inc(for_dve, 1)
            w.next(dg_ready)
            take(7)
            mm(ps[:, 7, 0:P], C("ones"), small[:, 2, :]).then_inc(for_dve, 1)
            w.next(dg_ready)
            take(6)
            mm(ps[:, 6, 0:P], C("ones"), small[:, 5, :]).then_inc(for_dve, 1)
            base = list(taken)
            with pe.Fori(0, NS // 2) as it:
                for r in range(2):
                    pe.wait_ge(bank_free[r], it + base[r])
                    for p in range(NPAGE):
                        n = r * NPAGE + p
                        pe.wait_ge(natp_in[n % NSLOT], it * (16 * 2 * NPAGE // NSLOT) + 16 * (n // NSLOT + 1))
                        pe.wait_ge(bank_free[2 + r], it + base[2 + r]) if p == 0 else None
                        for c in range(2):
                            last = mm(ps[:, 2 * c + r, 0:16], cpN[n % NSLOT][:, c * P:(c + 1) * P],
                                      PR[:, bass.ds(it * 2 * NPAGE + n, 1), :].rearrange("p o h -> p (o h)"),
                                      p == 0, p == NPAGE - 1)
                        last.then_inc(natp_used, 1)
            for b in range(4):
                taken[b] += NS // 2
            w.next(acc_ready)
            take(4)
            take(5)
            for h in range(HEADS):
                pr = slice(64 * (h % 2), 64 * (h % 2) + 64)
                o = ps[pr, 4 + h % 2, (h // 2) * NS:(h // 2 + 1) * NS]
                for c in range(2):
                    last = mm(o, w_uv[:, c, h * 64:(h + 1) * 64], accT[:, c, :, h], c == 0, c == 1)
            last.then_inc(for_dve, 1)
            w.next(oall_ready)
            project(TILES["mla_out"], 8, o_t)
            row_norm()
            peer(1)

        @block.vector
        def _(dve):
            w = Seen(dve)
            v = nc.vector
            steps = [0]

            def own(ins):
                steps[0] += 1
                ins.then_inc(dve_step, 1)
                dve.wait_ge(dve_step, steps[0])

            def tell(*sems):
                for s in sems:
                    dve.sem_inc(s, 1)

            def tt(out, a, b, op):
                return v.tensor_tensor(out, a, b, op)

            def root(x):
                v.reciprocal(x, x).then_inc(rsq_in, 1)
                w.next(rsq_out)

            def row_norm(gain):
                rs = rsb[:, 0:T]
                w.next(for_dve)
                own(v.tensor_scalar(rs, ps[:, 0, 0:T], 1.0 / D, EPS, ALU.mult, ALU.add))
                tell(bank_free[0])
                root(rs)
                for c in range(DC):
                    last = v.scalar_tensor_tensor(xn[:, c, :], xT[:, c, :], V(gain, c), rs, ALU.mult, ALU.mult)
                last.then_inc(xn_ready, 1)
                w.next(xn_ready)

            def take_sums(n, op):
                for i in range(n):
                    w.next(for_dve)
                    own(op(i))
                    tell(bank_free[i])

            def residual(first):
                for o in range(DC):
                    dve.wait_ge(tile_used, first + o + 1)
                    own(tt(xT[:, o, :], ps[:, o % 4, 0:T], xT[:, o, :], ALU.add))
                    tell(bank_free[o % 4])
                tell(x_added)

            def top16(rows):
                for vals, places, src, work in rows:
                    last = v.max(vals[:, 0:8], src)
                own(last)
                for vals, places, src, work in rows:
                    v.max_index(places[:, 0:8], vals[:, 0:8], src)
                    last = v.match_replace(work, vals[:, 0:8], src, VERY_NEG)
                own(last)
                for vals, places, src, work in rows:
                    last = v.max(vals[:, 8:16], work)
                own(last)
                for vals, places, src, work in rows:
                    last = v.max_index(places[:, 8:16], vals[:, 8:16], work)
                own(last)

            def choose_head(h):
                top16([(v16[0:nt, i, 2 * h + k], i16u[0:nt, i, 2 * h + k], S[0:nt, i, 2 * h + k], S2[0:nt, 2 * i + k])
                       for i, (t0, nt) in enumerate(TT) for k in range(2)])
                for i, (t0, nt) in enumerate(TT):
                    shape = [nt, TOPK, TOPK]
                    last = tt(cand[0:nt, i].rearrange("p (a b) -> p a b", a=TOPK),
                              v16[0:nt, i, 2 * h].unsqueeze(2).broadcast_to(shape),
                              v16[0:nt, i, 2 * h + 1].unsqueeze(1).broadcast_to(shape), ALU.add)
                own(last)
                top16([(ts16[0:nt, i, h], posu[0:nt, i, h], cand[0:nt, i], cand2[0:nt, i])
                       for i, (t0, nt) in enumerate(TT)])

            def gates():
                for i, (t0, nt) in enumerate(TT):
                    own(v.tensor_copy(i16f[0:nt, i], i16u[0:nt, i]))
                    best, pos = ts16[0:nt, i], posu[0:nt, i].rearrange("p h k -> p (h k)")
                    own(v.tensor_copy(smax[0:nt, i], best[:, :, 0:1]))
                    tt(best, best, smax[0:nt, i].broadcast_to([nt, PH, TOPK]), ALU.subtract).then_inc(gate_in, 1)
                    v.tensor_scalar(abu[0:nt, i, 0, :], pos, 4, None, ALU.logical_shift_right)
                    own(v.tensor_scalar(abu[0:nt, i, 1, :], pos, 15, None, ALU.bitwise_and))
                    own(v.tensor_copy(abf[0:nt, i], abu[0:nt, i]))

                def one_hot(e, i, k, nt):
                    return tt(e[0:nt].rearrange("p h (a b) -> p (h a) b", a=TOPK),
                              abf[0:nt, i, k, :].unsqueeze(2).broadcast_to([nt, P, TOPK]),
                              C("iota")[0:nt, 0:TOPK].unsqueeze(1).broadcast_to([nt, P, TOPK]), ALU.is_equal)

                def take(e, i, k, nt):
                    own(v.tensor_reduce(sel[0:nt, i, k, :], e[0:nt].rearrange("p h (a b) -> p (h a) b", a=TOPK), AX.X,
                                        ALU.add))

                def start(j):
                    one_hot(eqs[j % 2], *EQ_JOBS[j], P).then_inc(eq_made, 1)

                def finish(j):
                    w.next(eq_keys)
                    take(eqs[j % 2], *EQ_JOBS[j], P)

                def sample(k):
                    own(one_hot(eqs[2], 2, k, NS))
                    own(tt(eq_rows(eqs[2], NS), eq_rows(eqs[2], NS), key_of(2, k, NS), ALU.mult))
                    take(eqs[2], 2, k, NS)

                start(0)
                start(1)
                sample(0)
                finish(0)
                start(2)
                finish(1)
                start(3)
                sample(1)
                finish(2)
                finish(3)
                for i, (t0, nt) in enumerate(TT):
                    w.next(gate_exp)
                    best, sums = ts16[0:nt, i], smax[0:nt, i]
                    own(v.tensor_reduce(sums.rearrange("p h o -> p (h o)"), best, AX.X, ALU.add))
                    own(v.reciprocal(sums, sums))
                    tt(sel[0:nt, i, 2, :].rearrange("p (h k) -> p h k", h=PH), best,
                       sums.broadcast_to([nt, PH, TOPK]), ALU.mult).then_inc(sel_ready, 1)
                    w.next(sel_ready)

            def peer(layer):
                row_norm(f"norm_ffn{layer}")
                for h in range(PH):
                    w.next(s_copied, 2)
                    choose_head(h)
                gates()
                for i, (t0_, nt) in enumerate(TT):
                    w.next(for_dve)
                    own(v.tensor_copy(idx[:, :, t0_:t0_ + nt],
                                      ps[:, i, 0:3 * P].rearrange("p (k n) -> p k n", k=3)[:, :, 0:nt]))
                    tell(bank_free[i])
                own(v.tensor_copy(idxh[:, 0:3, :], idx))
                own(tt(rest, idx[:, 2, :], idxh[:, 2, :], ALU.subtract))
                own(v.tensor_copy(idxh[:, 3, :], rest))
                own(tt(rest, rest, idxh[:, 3, :], ALU.subtract))
                v.tensor_copy(idxh[:, 4, :], rest)
                own(v.tensor_copy(keys8, C("iota").unsqueeze(2).broadcast_to([P, P, OHT])))
                tell(idx_ready)
                w.next(xhi_ready)
                own(tt(x_lo[:, :], xnbuf[:, :], x_hi[:, :].bitcast(F32), ALU.subtract))
                for hf in range(2):
                    experts(layer, hf)
                dve.wait_ge(bank_free[7], marks[2 * layer + 1][7] + 2 * NG)
                tell(x_added)

            def experts(layer, hf):
                k = 2 * layer + hf
                sets0 = k * (T // OHT) + OHS * k
                with dve.Fori(0, T // OHT // OHS) as it:
                    for st in range(OHS):
                        these = lambda lo, n: idxh[:, lo:lo + n, bass.ds(it * (OHT * OHS) + st * OHT, OHT)]
                        dve.wait_ge(oh_used, it * OHS + (sets0 + st + 1))
                        tt(oh2[st], keys8[:, hf * HALF:(hf + 1) * HALF, :], these(1, 1).broadcast_to([P, HALF, OHT]),
                           ALU.is_equal).then_inc(oh2_made, 1)
                        tt(oh1[st], keys8, these(0, 1).broadcast_to([P, P, OHT]), ALU.is_equal)
                        dve.wait_ge(oh2_made, it * OHS + (k * (T // OHT) + st + 1))
                        tt(oh2g[st][:, 0:2], oh2[st].unsqueeze(1).broadcast_to([P, 2, HALF, OHT]),
                           these(2, 2).unsqueeze(2).broadcast_to([P, 2, HALF, OHT]), ALU.mult).then_inc(oh1_made, 1)
                base = marks[k]
                for b in range(OHS):
                    dve.wait_ge(bank_free[b], base[b])
                t0 = TILES[f"peer{layer}"] + 2 * HALF * hf
                fd = for_dve_before[k] = w.count(for_dve)

                def lower(at, u, it=0):
                    n = t0 + at + u
                    dve.wait_ge(hi_ready, it * 8 + (k * 4 * NG + at + u + 1))
                    s4 = (at + u) % 4
                    tt(w_half[1][s4], slot(n).rearrange("p c m -> p (c m)"), w_half[0][s4].bitcast(F32),
                       ALU.subtract).then_inc(tile_used, 1)

                def gate(g, it=0):
                    for u in range(GR):
                        b = 2 * (g % 2) + u
                        dve.wait_ge(bank_free[b], it + (base[b] + g // 2 + 1))
                        last = tt(hg[:, b, :], hg[:, b, :],
                                  G[:, bass.ds(it * (2 * GR) + (g * GR + u), 1), :].rearrange("p o t -> p (o t)"),
                                  ALU.mult)
                    last.then_inc(gated, 1)

                def hidden_lower(g, it=0):
                    dve.wait_ge(hhi_ready, it * 2 + (k * NG + g + 1))
                    two = slice(g % 2 * GR, g % 2 * GR + GR)
                    tt(h_half[1][:, two, :], hg[:, two, :], h_half[0][:, two, :].bitcast(F32), ALU.subtract
                       ).then_inc(h_ready, 1)

                def add(g, chunks, it=0):
                    for c in chunks:
                        dve.wait_ge(for_dve, it * 16 + (fd + DC * g + c + 1))
                        tt(xT[:, c, :], ps[:, 4 + c % 4, 0:T], xT[:, c, :], ALU.add).then_inc(bank_free[4 + c % 4], 1)

                for at in (0, 2):
                    for u in range(GR):
                        lower(at, u)
                gate(0)
                for u in range(GR):
                    lower(4, u)
                hidden_lower(0)
                with dve.Fori(0, NG // 2 - 1) as it:
                    for g in range(2):
                        add(g, (0,), it)
                        gate(g + 1, it)
                        add(g, (1, 2), it)
                        lower(4 * g + 6, 0, it)
                        add(g, (3, 4), it)
                        lower(4 * g + 6, 1, it)
                        add(g, (5,), it)
                        hidden_lower(g + 1, it)
                        add(g, (6, 7), it)
                        lower(4 * g + 8, 0, it)
                        lower(4 * g + 8, 1, it)
                add(NG - 2, range(4))
                gate(NG - 1)
                add(NG - 2, range(4, 8))
                hidden_lower(NG - 1)
                lower(4 * NG - 2, 0)
                lower(4 * NG - 2, 1)
                add(NG - 1, range(8))
                w.passed(for_dve, DC * NG)

            def sample_quarter(qd):
                st = st_q[qd % 2]
                rr, kr, vr_, kkr, br, dr = (smp_row[:, j, :] for j in range(6))
                row = lambda x: x.unsqueeze(1).broadcast_to([P, 16, 64])
                col = lambda x: x.unsqueeze(2).broadcast_to([P, 16, 64])
                dve.wait_ge(st_in[qd % 2], 16 * (qd // 2 + 1))
                own(tt(st_tmp, st, row(kkr), ALU.mult))
                own(v.tensor_reduce(skk, st_tmp, AX.X, ALU.add))
                own(tt(st, st, row(dr), ALU.mult))
                own(tt(st_tmp, col(skk), row(br), ALU.mult))
                own(tt(st, st, st_tmp, ALU.subtract))
                own(tt(st_tmp, col(vr_[:, 16 * qd:16 * qd + 16]), row(kr), ALU.mult))
                own(tt(st, st, st_tmp, ALU.add))
                own(tt(st_tmp, st, row(rr), ALU.mult))
                v.tensor_reduce(y_smp[:, 16 * qd:16 * qd + 16], st_tmp, AX.X, ALU.add).then_inc(st_done, 1)
                w.next(st_done)

            dve.wait_ge(consts_in, 16 * 7)
            row_norm("norm_mix0")
            tt(xx[:, :, 1:NP_], xn[:, :, 0:NP_ - 1], xn[:, :, 1:NP_], ALU.subtract)
            v.tensor_scalar(xx[:, :, 0:1], xn[:, :, 0:1], -1.0, None, ALU.mult)
            own(tt(xx[:, :, NP_:T], shift_sb, xn[:, :, NP_:T], ALU.subtract))
            users = [TILES["r"] + 8, TILES["k"] + 8, TILES["v"] + 8, TILES["w1"] + 1, TILES["a1"] + 1]
            for m, mu in enumerate([0, 2, 3, 1, 4, 5]):
                if m >= 2:
                    dve.wait_ge(tile_used, users[m - 2])
                for c in range(DC):
                    last = v.scalar_tensor_tensor(mix[m % 2][:, c, :], xx[:, c, :], V(f"mu{mu}", c), xn[:, c, :],
                                                  ALU.mult, ALU.add)
                last.then_inc(mix_ready, 1)
            w.next(proj_copied)
            v.tensor_scalar(ld_t, ld_t, -float(np.exp(-0.5)), None, ALU.mult).then_inc(ld_scaled, 1)
            own(tt(kk_t, k_t, vb("k_k"), ALU.mult))
            tt(tmp_t, kk_t, kk_t, ALU.mult).then_inc(stat_ready, 1)
            own(v.scalar_tensor_tensor(bon_t, a_t, -1.0, vb("k_a"), ALU.add, ALU.mult))
            own(v.scalar_tensor_tensor(k_t, bon_t, 1.0, k_t, ALU.add, ALU.mult))
            take_sums(DC, lambda i: v.tensor_scalar(bon_t[:, i, :], ps[:, i, 0:T], 1e-24, None, ALU.max))
            root(bon_t)
            own(tt(kk_t, kk_t, bon_t, ALU.mult))
            own(tt(a_t, a_t, kk_t, ALU.mult))
            own(tt(tmp_t, r_t, k_t, ALU.mult))
            tt(tmp_t, tmp_t, vb("r_k"), ALU.mult).then_inc(stat_ready, 1)
            for j, src in enumerate([r_t, k_t, v_t, kk_t, a_t]):
                last = v.tensor_copy(smp[:, j, :, :], src[:, :, NP_:T])
            own(last)
            w.next(smp_decay)
            tell(smp_ready)
            src = ld_t[:, :, 0:NP_]
            for lev in range(6):
                n = 1 << lev
                dst = cum[lev % 2]
                s4 = src.rearrange("p c (g t) -> p c g t", t=CH)
                d4 = dst.rearrange("p c (g t) -> p c g t", t=CH)
                v.tensor_copy(d4[:, :, :, 0:n], s4[:, :, :, 0:n])
                own(tt(d4[:, :, :, n:CH], s4[:, :, :, n:CH], s4[:, :, :, 0:CH - n], ALU.add))
                src = dst
            take_sums(DC, lambda i: tt(bon_t[:, i, :], ps[:, i, 0:T], v_t[:, i, :], ALU.mult))
            tt(Kb, cum[1], ld_t[:, :, 0:NP_], ALU.subtract).then_inc(cum_ready, 1)
            w.next(e_ready)
            own(v.tensor_copy(lam, Rb.rearrange("p c (g t) -> p c g t", t=CH)[:, :, :, CH - 1]))
            tt(Rb, Rb, r_t[:, :, 0:NP_], ALU.mult)
            tt(Kb, Kb, kk_t[:, :, 0:NP_], ALU.mult)
            own(tt(kb, Bb, k_t[:, :, 0:NP_], ALU.mult))
            tt(Bb, Bb, a_t[:, :, 0:NP_], ALU.mult).then_inc(ops_ready, 1)
            w.next(ops_ready)
            dve.wait_ge(smp_back, 16 * 6)

            def mask(m):
                return wm[:, m, :].unsqueeze(1).broadcast_to([P, 4, P])

            def mask2(m):
                return wm[:, m, :].unsqueeze(1).unsqueeze(1).broadcast_to([P, 2, 2, P])

            for c in range(DC):
                w.next(for_dve)
                own(v.tensor_copy(BKrow, ps[:, 1, :]))
                tell(rows_dve, bank_free[1])
                w.next(for_dve, 2)
                two = lambda x: x.rearrange("p (h n) -> p h n", h=2)
                own(v.tensor_copy(two(LT), ps[:, 2:4, 0:256]))
                hj = lambda x: x.rearrange("p (h j n) -> p h j n", h=2, j=2)
                hp = lambda x: x.rearrange("p h (j n) -> p h j n", j=2)
                tt(q4(NTl[0]), q4(LT), mask(2), ALU.mult).then_inc(nt_ready, 1)
                own(tt(hj(MTm), hp(ps[:, 2:4, 256:512]), mask2(0), ALU.mult))
                tell(bank_free[2], bank_free[3])
                tt(q4(NTl[1]), q4(LT), mask(3), ALU.mult).then_inc(nt_ready, 1)
                w.next(for_dve, 2)
                own(tt(hj(ArbT), hp(ps[:, 4:6, 0:256]), mask2(1), ALU.mult))
                own(tt(hj(ArkT), hp(ps[:, 4:6, 256:512]), mask2(1), ALU.mult))
                tell(ab_ready, bank_free[4], bank_free[5])
                for lev in range(6):
                    w.next(for_dve)
                    own(v.tensor_copy(XTs, ps[:, 3, :]))
                    tell(xt_ready)
                    if lev + 2 < 6:
                        tt(q4(NTl[lev % 2]), q4(LT), mask(2 + lev + 2), ALU.mult).then_inc(nt_ready, 1)
                tell(bank_free[3])
                if c % 2 == 1:
                    sample_quarter(c // 2)
                w.next(for_dve)
                own(tt(Rb[:, c, :], ps[:, 1, 0:NP_], Rb[:, c, :], ALU.add))
                own(v.tensor_copy(y_t[:, c, 0:NP_], ps[:, 4, 0:NP_]))
                for half in range(2):
                    pick = lambda x: x.rearrange("p (j f) k -> p j f k", f=2)[:, :, half, :]
                    own(tt(pick(ETi[:, c]), ps[:, 5 + half, 0:P].rearrange("p (j k) -> p j k", j=2),
                           C("stack")[:, 0:64].unsqueeze(1).broadcast_to([P, 2, 64]), ALU.add))
                    own(v.tensor_copy(pick(Hk[:, c]), ps[:, 5 + half, 256:256 + P].rearrange("p (j k) -> p j k", j=2)))
                tell(bank_free[1], bank_free[4], bank_free[5], bank_free[6], pair_done)
            lamb = lambda cc, rows=slice(0, P): lam[rows, :, cc].unsqueeze(2).broadcast_to([rows.stop - rows.start, DC, 64])
            tt(Pst, Hk[:, :, 0, :], lamb(0), ALU.mult).then_inc(state_ready, 1)
            w.next(state_ready)
            for cc in range(1, NCH):
                cols = slice(cc * 64, cc * 64 + 64)
                for h in range(2):
                    w.next(for_dve)
                    pr = slice(64 * h, 64 * h + 64)
                    own(tt(y_t[pr, :, cols], ps[pr, h, :].rearrange("p (c v) -> p c v", c=DC), y_t[pr, :, cols], ALU.add))
                    tell(bank_free[h])
                w.next(for_dve, 2)
                for h in range(2):
                    pr = slice(64 * h, 64 * h + 64)
                    own(tt(Pst[pr], ps[pr, 2 + h, :].rearrange("p (c v) -> p c v", c=DC), Hk[pr, :, cc, :], ALU.add))
                    tell(bank_free[2 + h])
                tt(Pst, Pst, lamb(cc), ALU.mult).then_inc(state_ready, 1)
                w.next(state_ready)
            w.next(for_dve)
            own(v.tensor_copy(y_t[:, :, NP_:T], ps[:, 4, 0:DC * NS].rearrange("p (c b) -> p c b", c=DC)))
            tell(bank_free[4], stat_ready)
            take_sums(DC, lambda i: v.scalar_tensor_tensor(y_t[:, i, :], ps[:, i, 0:T], -1.0 / 64, y_t[:, i, :],
                                                           ALU.mult, ALU.add))
            tt(tmp_t, y_t, y_t, ALU.mult).then_inc(stat_ready, 1)
            take_sums(DC, lambda i: v.tensor_scalar(kk_t[:, i, :], ps[:, i, 0:T], 1.0 / 64, GN_EPS, ALU.mult, ALU.add))
            root(kk_t)
            own(tt(y_t, y_t, kk_t, ALU.mult))
            for c in range(DC):
                last = v.tensor_scalar(y_t[:, c, :], y_t[:, c, :], V("ln_w", c), V("ln_b", c), ALU.mult, ALU.add)
            own(last)
            own(tt(y_t, y_t, bon_t, ALU.add))
            tt(y_t, y_t, g_t, ALU.mult).then_inc(yg_ready, 1)
            residual(TILES["rw_out"])
            peer(0)

            row_norm("norm_mix1")
            for i, n in enumerate((QL, KVL, ROPE)):
                w.next(for_dve)
                own(v.tensor_scalar(rsb[:, i * T:(i + 1) * T], ps[:, i, 0:T], 1.0 / n, EPS, ALU.mult, ALU.add))
                tell(bank_free[i])
            root(rsb[:, :])
            for c in range(3):
                v.scalar_tensor_tensor(cq[:, c, :], cq[:, c, :], V("q_norm", c), rsb[:, 0:T], ALU.mult, ALU.mult)
            for c in range(2):
                v.scalar_tensor_tensor(ckv[:, c, :], ckv[:, c, :], V("kv_norm", c), rsb[:, T:2 * T], ALU.mult, ALU.mult)
            own(v.scalar_tensor_tensor(kp, kp, V("kn_rope"), rsb[:, 2 * T:3 * T], ALU.mult, ALU.mult))
            tell(lat_ready)
            dve.wait_ge(mla_in, 32)
            w.next(for_dve)
            own(tt(sqb[:, 0, :], ps[:, 3, 0:T], cs[:, 1, :], ALU.mult))
            tell(bank_free[3])
            own(tt(kp, kp, cs[:, 0, :], ALU.mult))
            own(tt(kp, kp, sqb[:, 0, :], ALU.add))
            tell(kp_ready)
            w.next(proj_copied)
            for x, n, gain, size in ((qn, DC, "qn_nope", 64), (kn, DC, "kn_nope", 64), (qr, 4, "qn_rope", 32)):
                tt(sqb[:, 0:n, :], x, x, ALU.mult).then_inc(stat_ready, 1)
                take_sums(n, lambda i: v.tensor_scalar(rs8[:, i, :], ps[:, i, 0:T], 1.0 / size, EPS, ALU.mult, ALU.add))
                root(rs8[:, 0:n, :])
                own(v.scalar_tensor_tensor(x, x, V(gain), rs8[:, 0:n, :], ALU.mult, ALU.mult))
            tell(heads_ready)
            both = lambda x: x.unsqueeze(1).broadcast_to([P, 4, T])
            take_sums(4, lambda i: tt(sqb[:, i, :], ps[:, i, 0:T], cs[:, 1, :], ALU.mult))
            own(tt(qr, qr, both(cs[:, 0, :]), ALU.mult))
            own(tt(qr, qr, sqb[:, 0:4, :], ALU.add))
            tell(heads_ready)

            def masked_query(h):
                s = h % 2
                v.tensor_scalar(qm[s][:, 0, :], qn[:, h // 2, 0:NP_], C(f"half{h % 2}", 1), None, ALU.mult)
                v.tensor_scalar(qm[s][:, 1, :], qr[:, h // 4, 0:NP_], C(f"quar{h % 4}", 1), None, ALU.mult
                                ).then_inc(qm_ready, 1)

            masked_query(0)
            for i in range(HEADS + 1):
                if i < HEADS:
                    if i + 1 < HEADS:
                        masked_query(i + 1)
                    s = i % 2
                    w.next(for_dve)
                    own(v.scalar_tensor_tensor(Sm[s], ps[:, s, 0:3 * P], SCALE, C("amask", 3 * P), ALU.mult, ALU.add))
                    tell(bank_free[s])
                    v.tensor_reduce(mxl[s][:, 0:1], Sm[s][:, 0:P], AX.X, ALU.max)
                    own(v.tensor_reduce(mxl[s][:, 1:2], Sm[s][:, P:3 * P], AX.X, ALU.max))
                    v.tensor_scalar(mxl[s][:, 2:4], mxl[s][:, 0:2], -1.0, None, ALU.mult).then_inc(neg_ready, 1)
                if i >= 1:
                    h, s = i - 1, (i - 1) % 2
                    w.next(for_dve)
                    own(v.reciprocal(mxl[s][:, 6:8], mxl[s][:, 4:6]))
                    for j in range(2):
                        own(v.tensor_scalar(o_row[:, j, h * 64:(h + 1) * 64], ps[:, 4 + s, j * 64:(j + 1) * 64],
                                            mxl[s][:, 6 + j:7 + j], None, ALU.mult))
                    tell(bank_free[4 + s])
            tell(o_ready)
            qs, ks, rs_, kps = qn[:, :, NP_:T], kn[:, :, NP_:T], qr[:, :, NP_:T], kp[:, NP_:T]
            tt(prodn, qs, ks, ALU.mult)
            tt(prodr, rs_, kps.unsqueeze(1).broadcast_to([P, 4, NS]), ALU.mult)
            for h in range(2):
                v.tensor_scalar(qgm[:, :, h, :], qs, V("kn_nope"), C(f"half{h}", 1), ALU.mult, ALU.mult)
            for m in range(4):
                last = v.tensor_scalar(qrz.rearrange("p b (g m) -> p m g b", m=4)[:, m], rs_, C(f"quar{m}", 1), None,
                                       ALU.mult)
            own(last)
            tell(qs_ready)
            w.next(for_dve)
            for c in range(2):
                own(v.tensor_copy(qp[:, c].rearrange("p b h -> p h b"),
                                  ps[:, 0, c * P:(c + 1) * P].rearrange("p (h b) -> p h b", h=HEADS)))
            w.next(for_dve)
            own(v.tensor_scalar(small[:, 3, :].rearrange("p (b h) -> p h b", h=HEADS),
                                ps[:, 1, 0:P].rearrange("p (h b) -> p h b", h=HEADS), SCALE, None, ALU.mult))
            tell(bank_free[0], bank_free[1], qp_ready)
            w.next(ukhi_ready)
            own(tt(uk_half[1], w_uk, uk_half[0].bitcast(F32), ALU.subtract))
            tell(uk_ready)
            dve.sem_inc(sqp_used, 2)
            base = marks["pages"]

            def page_lower(n, it=0):
                dve.wait_ge(pghi_ready, it * 4 + (n + 1))
                tt(pg_half[1][:, n % 4], cpT[n % 4][:, 0:2, :], pg_half[0][:, n % 4].bitcast(F32), ALU.subtract
                   ).then_inc(pg_ready, 1)

            def page_sums(n, it):
                b = 2 * (n % 2)
                at = it * 4 + n
                dve.wait_ge(bank_free[b], it * 2 + (base[b] + n // 2 + 1))
                v.tensor_reduce(SS[:, bass.ds(at, 1), :].rearrange("p o h -> p (o h)"),
                                sqp[n % 2].rearrange("p (h d) -> p h d", h=HEADS), AX.X, ALU.add).then_inc(sqp_used, 1)
                dve.wait_ge(page_used, it * 4 + (n + 1))
                v.tensor_copy(SN[:, bass.ds(at, 1), :].rearrange("p o h -> p (o h)"), ps[:, 4 + n % 2, 0:32]
                              ).then_inc(bank_free[4 + n % 2], 1)

            page_lower(0)
            page_lower(1)
            with dve.Fori(0, PAGES // 4 - 1) as it:
                for n in range(4):
                    page_lower(n + 2, it)
                    page_sums(n, it)
            for n in range(4):
                if n < 2:
                    page_lower(n + 2, PAGES // 4 - 1)
                page_sums(n, PAGES // 4 - 1)
            dve.wait_ge(bank_free[5], base[5] + PAGES // 2)
            own(v.tensor_scalar(SS, SS, 1.0 / 64, EPS, ALU.mult, ALU.add))
            root(SS)
            own(v.scalar_tensor_tensor(PR, SN[:, :, 0:16], SCALE, SS, ALU.mult, ALU.mult))
            own(v.scalar_tensor_tensor(PR, SN[:, :, 16:32], SCALE, PR, ALU.mult, ALU.add))
            by_req = lambda x: x.rearrange("p (b g) h -> p b h g", b=NS)
            bh = lambda i: small[:, i, :].rearrange("p (b h) -> p b h", b=NS)
            own(v.tensor_reduce(bh(0), by_req(PR), AX.X, ALU.max))
            tell(m1_ready)
            w.next(for_dve)
            own(v.tensor_reduce(small[:, 1, 0:1], ps[:, 6, 0:P], AX.X, ALU.max))
            own(v.tensor_scalar(small[:, 2, :], C("ident"), small[:, 1, 0:1], None, ALU.mult))
            tell(bank_free[6], dg_ready)
            w.next(for_dve)
            own(tt(small[:, 4, :], ps[:, 7, 0:P], small[:, 3, :], ALU.max))
            tell(bank_free[7])
            PR4 = PR.rearrange("p (b g) h -> p b g h", b=NS)
            tt(PR4, PR4, bh(4).unsqueeze(2).broadcast_to([P, NS, NPAGE, HEADS]), ALU.subtract)
            own(tt(small[:, 3, :], small[:, 3, :], small[:, 4, :], ALU.subtract))
            tell(pr_in)
            w.next(pr_exp)
            own(v.tensor_reduce(bh(5), by_req(PR), AX.X, ALU.add))
            tell(dg_ready)
            w.next(for_dve)
            own(tt(small[:, 6, :], ps[:, 6, 0:P], small[:, 3, :], ALU.add))
            tell(bank_free[6])
            own(v.reciprocal(small[:, 6, :], small[:, 6, :]))
            with dve.Fori(0, NS // 2) as it:
                for r in range(2):
                    dve.wait_ge(natp_used, it * 32 + 16 * (r + 1))
                    for c in range(2):
                        v.tensor_copy(accT[:, c, bass.ds(it * 2 + r, 1), :].rearrange("p o h -> p (o h)"),
                                      ps[:, 2 * c + r, 0:16]).then_inc(bank_free[2 * c + r], 1)
            new = ckv[:, :, NP_:T].unsqueeze(3).broadcast_to([P, 2, NS, HEADS])
            for c in range(2):
                own(tt(cnew[:, c], new[:, c], bh(3), ALU.mult))
                own(tt(accT[:, c], accT[:, c], cnew[:, c], ALU.add))
                own(tt(accT[:, c], accT[:, c], bh(6), ALU.mult))
            tell(acc_ready)
            w.next(for_dve)
            for h in range(2):
                pr = slice(64 * h, 64 * h + 64)
                own(v.tensor_copy(o_t[pr, :, NP_:T], ps[pr, 4 + h, 0:DC * NS].rearrange("p (c b) -> p c b", c=DC)))
            tell(bank_free[4], bank_free[5])
            w.next(oT_copied)
            tell(oall_ready)
            residual(TILES["mla_out"])
            peer(1)

        @block.scalar
        def _(act):
            w = Seen(act)
            steps = [0]

            def own(ins):
                steps[0] += 1
                ins.then_inc(act_step, 1)
                act.wait_ge(act_step, steps[0])

            def fn(out, in_, func=ACT.Copy, **kw):
                return nc.scalar.activation(out, in_, func, **kw)

            def tell(*sems):
                for s in sems:
                    act.sem_inc(s, 1)

            def row_norm():
                fn(xnbuf[:, :], xbuf[:, :], ACT.Square).then_inc(sq_ready, 1)
                root(rsb[:, 0:T])

            def root(x):
                w.next(rsq_in)
                fn(x, x, ACT.Sqrt).then_inc(rsq_out, 1)

            def peer(layer):
                w.next(x_added)
                row_norm()
                first = TILES[f"wq{layer}"]
                if layer == 0:
                    act.wait_ge(wkv_sent, 16)
                else:
                    act.wait_ge(lat_sent, 32)
                for g in range(17):
                    if g < 16:
                        act.wait_ge(tile_used, first + g + 1)
                        own(fn(qb[g % 2], ps[:, g % 2, 0:T]))
                        tell(q_copied, bank_free[g % 2])
                    if g >= 1:
                        w.next(for_act)
                        b = 2 + g % 2
                        own(fn(S[:, 0:2, g - 1, :], ps[:, b, 0:2 * P].rearrange("p (i n) -> p i n", i=2)))
                        own(fn(S[0:NS, 2, g - 1, :], ps[0:NS, b, 2 * P:3 * P]))
                        tell(bank_free[b], s_copied)
                for i, (t0, nt) in enumerate(TT):
                    w.next(gate_in)
                    fn(ts16[0:nt, i], ts16[0:nt, i], ACT.Exp).then_inc(gate_exp, 1)
                w.next(idx_ready)
                fn(x_hi[:, :], xnbuf[:, :]).then_inc(xhi_ready, 1)
                for hf in range(2):
                    experts(layer, hf)

            def experts(layer, hf):
                k = 2 * layer + hf
                sets0 = k * (T // OHT) + OHS * (k + 1)
                with act.Fori(0, T // OHT // OHS) as it:
                    for st in range(OHS):
                        act.wait_ge(oh_used, it * OHS + (sets0 + st + 1))
                        fn(G[:, :, bass.ds(it * (OHT * OHS) + st * OHT, OHT)],
                           ps[:, st, :].rearrange("p (t n) -> p n t", t=OHT)).then_inc(bank_free[st], 1)
                t0 = TILES[f"peer{layer}"] + 2 * HALF * hf
                fa, fd = w.count(for_act), for_dve_before[k]

                def upper(at, it=0):
                    for u in range(GR):
                        n = t0 + at + u
                        act.wait_ge(slot_in[n % RING], it * 16 + 16 * (n // RING + 1))
                        fn(w_half[0][(at + u) % 4], slot(n).rearrange("p c m -> p (c m)")).then_inc(hi_ready, 1)

                def gelu(g, it=0):
                    for u in range(GR):
                        act.wait_ge(for_act, it * 4 + (fa + 2 * g + u + 1))
                        b = 2 * (g % 2) + u
                        fn(hg[:, b, :], ps[:, b, 0:T], ACT.Gelu_apprx_tanh).then_inc(bank_free[b], 1)

                def hidden_upper(g, it=0):
                    act.wait_ge(gated, it * 2 + (k * NG + g + 1))
                    two = slice(g % 2 * GR, g % 2 * GR + GR)
                    fn(h_half[0][:, two, :], hg[:, two, :]).then_inc(hhi_ready, 1)

                act.wait_ge(for_dve, fd)
                upper(0)
                upper(2)
                gelu(0)
                upper(4)
                hidden_upper(0)
                with act.Fori(0, NG // 2 - 1) as it:
                    for g in range(2):
                        gelu(g + 1, it)
                        upper(4 * g + 6, it)
                        hidden_upper(g + 1, it)
                        act.wait_ge(for_dve, it * 16 + (fd + DC * (g + 1)))
                        upper(4 * g + 8, it)
                gelu(NG - 1)
                hidden_upper(NG - 1)
                upper(4 * NG - 2)
                w.passed(for_act, 2 * NG)

            act.wait_ge(consts_in, 16 * 7)
            row_norm()
            for name, dst in (("r", r_t), ("k", k_t), ("v", v_t)):
                for o in range(DC):
                    act.wait_ge(tile_used, TILES[name] + o + 1)
                    fn(dst[:, o, :], ps[:, o % 4, 0:T]).then_inc(bank_free[o % 4], 1)
            for m, (name, dst, f, rows) in enumerate([("w1", lw, ACT.Tanh, 64), ("a1", la, ACT.Copy, 64),
                                                      ("g1", lg, ACT.Sigmoid, 128)]):
                act.wait_ge(tile_used, TILES[name] + 1)
                own(fn(dst[0:rows, :], ps[0:rows, m, 0:T], f))
                tell(lora_ready, bank_free[m])
            for name, dst in (("w2", ld_t), ("a2", a_t), ("g2", g_t)):
                for o in range(DC):
                    if o == DC - 1:
                        act.wait_ge(tile_used, TILES[name] + 1)
                    else:
                        w.next(for_act)
                    src = ps[:, o % 4, 0:T]
                    if name == "g2":
                        own(fn(dst[:, o, :], src))
                    else:
                        own(fn(dst[:, o, :], src, ACT.Sigmoid, bias=V("w0" if name == "w2" else "a0", o)))
                    tell(bank_free[o % 4])
            tell(proj_copied)
            w.next(ld_scaled)
            fn(smp[:, 5, :, :], ld_t[:, :, NP_:T], ACT.Exp).then_inc(smp_decay, 1)
            root(bon_t)
            for j in range(6):
                for half in range(2):
                    b = (2 * j + half) % 4
                    w.next(for_act)
                    own(fn(rows_sb[j // 2][:, (j % 2) * D + half * 512:(j % 2) * D + half * 512 + 512], ps[0:NS, b, :]))
                    tell(smp_rows, bank_free[b])
            act.wait_ge(smp_out, 48)
            w.next(cum_ready)
            fn(Rb, cum[1], ACT.Exp)
            fn(Kb, Kb, ACT.Exp)
            fn(Bb, cum[1], ACT.Exp, scale=-1.0).then_inc(e_ready, 1)
            for c in range(DC):
                w.next(for_act)
                rows = ps[:, 0, :].rearrange("p (i j h n) -> p i j h n", i=2, j=2, h=2)
                own(fn(Vrow, rows[:, 0]))
                own(fn(RHS.rearrange("p (h j n) -> p j h n", h=2, j=2)[:, :, :, 0:64], rows[:, 1]))
                tell(rows_act, bank_free[0])
                w.next(for_act)
                own(fn(q4(RHS)[:, :, 64:128], ps[:, 6, 0:256].rearrange("p (q n) -> p q n", q=4)))
                tell(rhs_ready, bank_free[6])
                w.next(for_act)
                fn(Xs, ps[:, 2, :]).then_inc(x_ready, 1)
                for lev in range(1, 6):
                    w.next(for_act)
                    own(fn(Zs, ps[:, 7, :]))
                    tell(z_ready, bank_free[7])
                    w.next(for_act)
                    if lev < 5:
                        fn(Xs, ps[:, 2, :]).then_inc(x_ready, 1)
                tell(bank_free[2])
                w.next(for_act)
                own(fn(nWU, ps[:, 0, :], ACT.Copy, scale=-1.0))
                tell(nwu_ready, bank_free[0])
            root(kk_t)
            act.wait_ge(shift_sent, 16)
            peer(0)

            w.next(x_added)
            row_norm()
            for o in range(6):
                act.wait_ge(tile_used, TILES["mla_in"] + o + 1)
                dst = cq[:, o, :] if o < 3 else ckv[:, o - 3, :] if o < 5 else kp
                own(fn(dst, ps[:, o % 4, 0:T]))
                tell(bank_free[o % 4])
            fn(sqb[:, 0:3, :], cq, ACT.Square)
            fn(sqb[:, 3:5, :], ckv, ACT.Square)
            fn(sqb[:, 5, :], kp, ACT.Square).then_inc(sq_ready, 1)
            root(rsb[:, :])
            for o in range(12):
                act.wait_ge(tile_used, TILES["qb"] + o + 1)
                own(fn(qn[:, o, :] if o < 8 else qr[:, o - 8, :], ps[:, o % 4, 0:T]))
                tell(bank_free[o % 4])
            for o in range(DC):
                w.next(for_act)
                own(fn(kn[:, o, :], ps[:, o % 4, 0:T]))
                tell(bank_free[o % 4])
            for j in range(2):
                for half in range(2):
                    w.next(for_act)
                    own(fn(vr[:, j, half * 512:(half + 1) * 512], ps[:, 2 * j + half, :]))
                    tell(bank_free[2 * j + half])
            tell(proj_copied)
            root(rs8)
            root(rs8)
            root(rs8[:, 0:4, :])
            for i in range(HEADS + 1):
                if i < HEADS:
                    s = i % 2
                    w.next(neg_ready)
                    fn(Sm[s][:, 0:P], Sm[s][:, 0:P], ACT.Exp, bias=mxl[s][:, 2:3], accum_out=mxl[s][:, 4:5])
                    own(fn(Sm[s][:, P:3 * P], Sm[s][:, P:3 * P], ACT.Exp, bias=mxl[s][:, 3:4],
                           accum_out=mxl[s][:, 5:6]))
                    tell(p_ready)
                if i >= 1:
                    s = (i - 1) % 2
                    w.next(for_act)
                    own(fn(PTs[s], ps[:, 2 + s, 0:3 * P]))
                    tell(pt_ready, bank_free[2 + s])
            for j in range(2):
                for half in range(2):
                    w.next(for_act)
                    own(fn(o_t[:, half * 4:half * 4 + 4, j * P:(j + 1) * P],
                           ps[:, 2 * j + half, :].rearrange("p (c n) -> p c n", c=4)))
                    tell(bank_free[2 * j + half])
            tell(oT_copied)
            w.next(qs_ready)
            fn(uk_hi[:, :].rearrange("p (c n) -> p c n", c=2), w_uk).then_inc(ukhi_ready, 1)
            fa = w.count(for_act)

            def page_upper(n, it=0):
                act.wait_ge(page_in[n % 4], it * 16 + 16 * (n // 4 + 1))
                fn(pg_half[0][:, n % 4], cpT[n % 4][:, 0:2, :]).then_inc(pghi_ready, 1)

            def squares(n, it):
                b = 2 * (n % 2)
                act.wait_ge(for_act, it * 4 + (fa + n + 1))
                act.wait_ge(sqp_used, it * 4 + (n + 1))
                fn(sqp[n % 2].rearrange("p (a n) -> p a n", a=2), ps[:, b:b + 2, :], ACT.Square
                   ).then_inc(bank_free[b], 1)

            page_upper(0)
            page_upper(1)
            with act.Fori(0, PAGES // 4 - 1) as it:
                for n in range(4):
                    page_upper(n + 2, it)
                    squares(n, it)
            for n in range(4):
                if n < 2:
                    page_upper(n + 2, PAGES // 4 - 1)
                squares(n, PAGES // 4 - 1)
            w.passed(for_act, PAGES)
            for n in (n for n in range(NSLOT) if n not in POOL_SLOTS):
                page(act, cache_n, n, cpN[n], natp_in[n])
            root(SS)
            w.next(pr_in)
            fn(PR, PR, ACT.Exp)
            fn(small[:, 3, :], small[:, 3, :], ACT.Exp).then_inc(pr_exp, 1)
            with act.Fori(1, PAGES // NSLOT) as it:
                for n in (n for n in range(NSLOT) if n not in POOL_SLOTS):
                    act.wait_ge(natp_used, it * NSLOT + (n + 1 - NSLOT))
                    page(act, cache_n, it * NSLOT + n, cpN[n], natp_in[n])
            peer(1)


def kernel(**inputs):
    import concourse.bacc as _bacc
    from concourse.bass_utils import run_bass_kernel_spmd as _run

    f = {k: np.asarray(a) for k, a in inputs.items()}
    con = np.ascontiguousarray

    def chunks(x):
        return con(x.T.reshape(DC, P, -1).transpose(1, 0, 2))

    def tiles(wt, cols=P):
        k, m = wt.shape
        out = np.zeros((m // cols, P, DC, P), np.float32)
        out[:, :, :k // P, :cols] = wt.reshape(k // P, P, m // cols, cols).transpose(2, 1, 0, 3)
        return out.reshape(-1, P, D)

    def hidden_rows(wt):
        out = np.zeros((1, P, D), np.float32)
        out[0, :wt.shape[0]] = wt
        return out

    def experts(u, vt):
        ut = u.reshape(P, P, DC, P).transpose(1, 3, 2, 0).reshape(P, P, D)
        vt = vt.reshape(P, P, D).transpose(1, 0, 2)
        out = []
        for lo in (0, HALF):
            out.append(ut[lo:lo + GR])
            for g in range(lo + GR, lo + HALF, GR):
                out += [ut[g:g + GR], vt[g - GR:g]]
            out.append(vt[lo + HALF - GR:lo + HALF])
        return out

    x_t = chunks(np.concatenate([f["x_prompt"][0], f["x_sample"][:, 0]], 0))
    shift_t = chunks(f["state_shift"][0])
    vs = {"norm_mix0": f["norm_mix"][0], "norm_mix1": f["norm_mix"][1], "norm_ffn0": f["norm_ffn"][0],
          "norm_ffn1": f["norm_ffn"][1], "w0": f["rw_w0"], "a0": f["rw_a0"], "k_k": f["rw_k_k"], "k_a": f["rw_k_a"],
          "r_k": f["rw_r_k"], "ln_w": f["rw_ln_w"], "ln_b": f["rw_ln_b"]}
    for m in range(6):
        vs[f"mu{m}"] = f["rw_mu"][0, m]
    vecs = [vs[n].reshape(DC, P).T for n in VECS]
    vecs += [f["mla_q_norm"].reshape(3, P).T, f["mla_kv_norm"].reshape(2, P).T]
    for n, rep in (("mla_qn_nope", 2), ("mla_qn_rope", 4), ("mla_kn_nope", 2), ("mla_kn_rope", 4)):
        vecs.append(np.tile(f[n][0], rep)[:, None])
    vecs = con(np.concatenate(vecs, 1))
    consts, wmasks, rope = const_arrays()

    w_in = f["mla_w_in"][0]
    w_in = np.concatenate([w_in[:, :QL + KVL], np.tile(w_in[:, QL + KVL:], (1, 4))], 1)
    w_qb = f["mla_w_qb"][0].reshape(QL, HEADS, 96)
    w_qb = np.concatenate([w_qb[:, :, :64].reshape(QL, D), w_qb[:, :, 64:].reshape(QL, 512)], 1)
    parts = [tiles(f["rw_w_in"][0, m]) for m in range(3)]
    parts += [tiles(f["rw_w1"][0], 64), tiles(f["rw_a1"][0], 64), tiles(f["rw_g1"][0])]
    parts += [hidden_rows(f["rw_w2"][0]), hidden_rows(f["rw_a2"][0]), hidden_rows(f["rw_g2"][0])]
    parts += [tiles(f["rw_w_out"][0]), tiles(f["peer_w_q"][0])] + experts(f["peer_u"][0], f["peer_v"][0])
    parts += [tiles(w_in), tiles(w_qb), tiles(f["mla_w_out"][0]), tiles(f["peer_w_q"][1])]
    parts += experts(f["peer_u"][1], f["peer_v"][1])
    wstream = np.concatenate(parts, 0)
    assert wstream.shape[0] == NTILES

    sub_keys = con(f["peer_sub_keys"].transpose(3, 0, 1, 2).reshape(P, 4 * P))
    kvb = f["mla_w_kvb"][0].reshape(KVL, HEADS, 128)
    w_uk, w_uv = kvb[:, :, :64].reshape(KVL, D), kvb[:, :, 64:].reshape(KVL, D)
    mla_w = con(np.concatenate([w_uk.reshape(2, P, D).transpose(1, 0, 2).reshape(P, -1),
                                w_uv.reshape(2, P, D).transpose(1, 0, 2).reshape(P, -1),
                                w_uk.T.reshape(DC, P, KVL).transpose(1, 0, 2).reshape(P, -1)], 1))
    ckv_pool = f["cache_ckv"][0]
    cache_t = con(np.concatenate([ckv_pool.transpose(0, 2, 1).reshape(POOL, 2, P, P).transpose(0, 2, 1, 3),
                                  np.tile(f["cache_kpe"][0].transpose(0, 2, 1), (1, 4, 1))[:, :, None, :]], 2)
                  ).reshape(POOL, P, 3 * P)
    state = con(f["state_wkv"][0].reshape(P, 64 * 64))
    page_table = con(f["page_table"].reshape(1, PAGES))

    ins = {"x_t": x_t.reshape(P, -1), "shift_t": shift_t, "vecs": vecs, "consts": consts, "wmasks": wmasks,
           "rope": rope, "wstream": wstream, "sub_keys": sub_keys, "mla_w": mla_w, "page_table": page_table,
           "cache_t": cache_t, "cache_n": con(ckv_pool), "state": state}
    outs = {"y": (P, DC * T), "ckv": (P, 2, T), "kpe": (ROPE, T), "wkv_p": (P, DC, 64), "shift": (P, DC, NS + 1),
            "wkv_s": (P, 64 * 64)}
    nc = _bacc.Bacc("TRN2", target_bir_lowering=False, num_devices=1)
    args, arrays = [], {}
    for n, a in ins.items():
        arrays[f"in_{n}"] = a
        args.append(nc.dram_tensor(f"in_{n}", a.shape, mybir.dt.from_np(a.dtype), kind="ExternalInput").ap())
    for n, shape in outs.items():
        args.append(nc.dram_tensor(f"out_{n}", shape, F32, kind="ExternalOutput").ap())
    build(nc, *args)
    r = _run(nc, [arrays], core_ids=[0]).results[0]
    got = {n: r[f"out_{n}"] for n in outs}
    y = got["y"].reshape(P, DC, T).transpose(2, 1, 0).reshape(T, D)
    ckv = got["ckv"].transpose(2, 1, 0).reshape(T, KVL)
    kpe = got["kpe"].T
    shift = got["shift"].transpose(2, 1, 0).reshape(NS + 1, D)
    wkv_p = got["wkv_p"].reshape(2, 64, DC, 64).transpose(2, 0, 3, 1).reshape(HEADS, 64, 64)
    c = con
    return (c(y[:NP_])[None], c(y[NP_:])[:, None], c(ckv[:NP_])[None, None], c(kpe[:NP_])[None, None],
            c(wkv_p)[None, None], c(shift[:1])[None], c(ckv[NP_:])[None, :, None], c(kpe[NP_:])[None, :, None],
            c(got["wkv_s"].reshape(1, NS, HEADS, 64, 64)), c(shift[1:])[None])
```
